# Optimizing a Trainium2 kernel written in Bass

```python
import math
import jax, jax.numpy as jnp
from jax import lax
import numpy as np

D_MODEL = 1024
BATCH = 1
SEQ = 1024
DEPTH = 1

ATTN_HEADS = 4
HEAD_DIM = 64
V_DIM = 2 * HEAD_DIM
ATTN_WIDTH = ATTN_HEADS * V_DIM
QK_WIDTH = ATTN_HEADS * 2 * HEAD_DIM
POOL_WINDOWS = (2, 4, 8, 16)
POOL_GROUPS = len(POOL_WINDOWS)
POOL_GROUP_DIM = 128
POOL_WIDTH = POOL_GROUPS * POOL_GROUP_DIM
N_BRANCHES = 2
GATE_WIDTH = N_BRANCHES * D_MODEL
IN_COLS = 2 * QK_WIDTH + ATTN_WIDTH + POOL_WIDTH + GATE_WIDTH
D_FF = 4 * D_MODEL
BLOCK_Q = 128
EPS = 1e-6
NEG_BIG = -1e30

kernel_name = "hybrid_diffattn_pool_gated_block"

def rms_norm(x, g):
    xf = x.astype(jnp.float32)
    y = xf * lax.rsqrt(jnp.mean(xf * xf, axis=-1, keepdims=True) + EPS)
    return (y * g.astype(jnp.float32)).astype(x.dtype)

def lambda_init_fn(layer_idx):
    return 0.8 - 0.6 * math.exp(-0.3 * layer_idx)

def diff_attention(q, k, v, lam):
    B, S, H, _, d = q.shape
    nb = S // BLOCK_Q
    qh = q.transpose(0, 2, 3, 1, 4)
    kh = k.transpose(0, 2, 3, 1, 4)
    vh = v.transpose(0, 2, 1, 3)
    qb = qh.reshape(B, H, 2, nb, BLOCK_Q, d).transpose(3, 0, 1, 2, 4, 5)
    k_pos = jnp.arange(S)
    scale = d ** -0.5

    def one_block(args):
        q_blk, start = args
        s = jnp.einsum('bhcqd,bhckd->bhcqk', q_blk, kh).astype(jnp.float32) * scale
        q_pos = start + jnp.arange(BLOCK_Q)
        mask = k_pos[None, :] <= q_pos[:, None]
        s = jnp.where(mask, s, NEG_BIG)
        p = jax.nn.softmax(s, axis=-1)
        w = p[:, :, 0] - lam * p[:, :, 1]
        return jnp.einsum('bhqk,bhke->bhqe', w.astype(vh.dtype), vh)

    starts = jnp.arange(nb) * BLOCK_Q
    out = lax.map(one_block, (qb, starts))
    return out.transpose(1, 0, 3, 2, 4).reshape(B, S, H, 2 * d)

def causal_pool_mixer(xp, pool_w, pool_scale):
    B, S, _ = xp.shape
    xg = xp.reshape(B, S, POOL_GROUPS, POOL_GROUP_DIM)
    xf = xg.astype(jnp.float32)
    c0 = jnp.concatenate([jnp.zeros((B, 1, POOL_GROUPS, POOL_GROUP_DIM), jnp.float32),
                          jnp.cumsum(xf, axis=1)], axis=1)
    upper = c0[:, 1:]
    t1 = jnp.arange(1, S + 1, dtype=jnp.float32)
    outs = []
    for g, w in enumerate(POOL_WINDOWS):
        lower = jnp.concatenate([jnp.zeros((B, w - 1, POOL_GROUP_DIM), jnp.float32),
                                 c0[:, :S - w + 1, g]], axis=1)
        count = jnp.minimum(t1, float(w))[None, :, None]
        outs.append((upper[:, :, g] - lower) / count - xf[:, :, g])
    pooled = jnp.stack(outs, axis=2).astype(xp.dtype)
    mixed = jnp.einsum('bsgc,gcd->bsgd', pooled, pool_w)
    return mixed.reshape(B, S, POOL_WIDTH) * pool_scale

def setup_inputs(seed: int = 0) -> dict:
    key = jax.random.key(seed)
    ks = jax.random.split(key, 20)
    f = jnp.float32
    nrm = lambda k, shape, s: jax.random.normal(k, shape, f) * s
    return {
        "x": jax.random.normal(ks[0], (BATCH, SEQ, D_MODEL), f),
        "norm1_g": 1.0 + nrm(ks[1], (DEPTH, D_MODEL), 0.1),
        "w_in": nrm(ks[2], (DEPTH, D_MODEL, IN_COLS), D_MODEL ** -0.5),
        "b_gate": nrm(ks[3], (DEPTH, GATE_WIDTH), 0.1),
        "q_norm_g": 1.0 + nrm(ks[4], (DEPTH, HEAD_DIM), 0.1),
        "k_norm_g": 1.0 + nrm(ks[5], (DEPTH, HEAD_DIM), 0.1),
        "lam_params": nrm(ks[6], (DEPTH, 4, HEAD_DIM), 0.1),
        "subln_g": 1.0 + nrm(ks[7], (DEPTH, V_DIM), 0.1),
        "pool_w": nrm(ks[8], (DEPTH, POOL_GROUPS, POOL_GROUP_DIM, POOL_GROUP_DIM), POOL_GROUP_DIM ** -0.5),
        "pool_scale": 1.0 + nrm(ks[9], (DEPTH, POOL_WIDTH), 0.1),
        "w_up_attn": nrm(ks[10], (DEPTH, ATTN_WIDTH, D_MODEL), ATTN_WIDTH ** -0.5),
        "w_up_pool": nrm(ks[11], (DEPTH, POOL_WIDTH, D_MODEL), POOL_WIDTH ** -0.5),
        "w_o": nrm(ks[12], (DEPTH, D_MODEL, D_MODEL), D_MODEL ** -0.5),
        "norm2_g": 1.0 + nrm(ks[13], (DEPTH, D_MODEL), 0.1),
        "w_mlp_in": nrm(ks[14], (DEPTH, D_MODEL, D_FF), D_MODEL ** -0.5),
        "w_mlp_out": nrm(ks[15], (DEPTH, D_FF, D_MODEL), D_FF ** -0.5),
    }

def reference(x, norm1_g, w_in, b_gate, q_norm_g, k_norm_g, lam_params, subln_g,
              pool_w, pool_scale, w_up_attn, w_up_pool, w_o, norm2_g, w_mlp_in, w_mlp_out):
    B, S, _ = x.shape
    c_q = QK_WIDTH
    c_k = c_q + QK_WIDTH
    c_v = c_k + ATTN_WIDTH
    c_p = c_v + POOL_WIDTH
    for l in range(DEPTH):
        lam_init = lambda_init_fn(l)
        h = rms_norm(x, norm1_g[l])
        proj = jnp.einsum('bsd,dc->bsc', h, w_in[l])
        q = proj[..., :c_q].reshape(B, S, ATTN_HEADS, 2, HEAD_DIM)
        k = proj[..., c_q:c_k].reshape(B, S, ATTN_HEADS, 2, HEAD_DIM)
        v = proj[..., c_k:c_v].reshape(B, S, ATTN_HEADS, V_DIM)
        xp = proj[..., c_v:c_p]
        gates = jax.nn.sigmoid(proj[..., c_p:] + b_gate[l]).reshape(B, S, N_BRANCHES, D_MODEL)

        q = rms_norm(q, q_norm_g[l])
        k = rms_norm(k, k_norm_g[l])
        lp = lam_params[l].astype(jnp.float32)
        lam = (jnp.exp(jnp.sum(lp[0] * lp[1])) - jnp.exp(jnp.sum(lp[2] * lp[3]))
               + lam_init)
        a = diff_attention(q, k, v, lam)
        a = rms_norm(a, subln_g[l]) * (1.0 - lam_init)
        y_attn = jnp.einsum('bsa,ad->bsd', a.reshape(B, S, ATTN_WIDTH), w_up_attn[l])

        p = causal_pool_mixer(xp, pool_w[l], pool_scale[l])
        y_pool = jnp.einsum('bsp,pd->bsd', p, w_up_pool[l])

        merged = gates[:, :, 0] * y_attn + gates[:, :, 1] * y_pool
        x = x + jnp.einsum('bsd,de->bse', merged, w_o[l])

        h2 = rms_norm(x, norm2_g[l])
        u = jnp.square(jax.nn.relu(jnp.einsum('bsd,df->bsf', h2, w_mlp_in[l])))
        x = x + jnp.einsum('bsf,fd->bsd', u, w_mlp_out[l])
    return x


_drawn_inputs = setup_inputs


def setup_inputs(seed=0):
    import zlib

    import numpy as np

    out = dict(_drawn_inputs(seed))
    spreads = {}
    factors = {}
    for name, (base, spread) in spreads.items():
        noise = np.random.default_rng([zlib.crc32(name.encode()), seed]).standard_normal(out[name].shape)
        drawn = base * np.exp(spread * noise) if base else spread * noise
        out[name] = __import__('jax').numpy.asarray(drawn.astype(out[name].dtype))
    for name, factor in factors.items():
        out[name] = (out[name] * factor).astype(out[name].dtype)
    return out
```

```python
from contextlib import ExitStack

import concourse.bass as bass
from concourse import mybir

F32 = mybir.dt.float32
F32R = mybir.dt.float32r
ALU = mybir.AluOpType
ACT = mybir.ActivationFunctionType
AX = mybir.AxisListType

P = 128
KB = 1024


def trunk_layer(nc, x, norm1_g, w_in, b_gate, q_norm_g, k_norm_g, lam_params, subln_g,
                pool_w, pool_scale, w_up_attn, w_up_pool, w_o, norm2_g, w_mlp_in, w_mlp_out, y):
    _, SEQ, D = x.shape
    HEAD = q_norm_g.shape[1]
    VDIM = subln_g.shape[1]
    HEADS = w_up_attn.shape[1] // VDIM
    GROUPS = pool_w.shape[1]
    FF = w_mlp_in.shape[2]
    assert SEQ == D == 1024 and 2 * HEAD == VDIM == P and GROUPS == HEADS == 4
    EPS = 1e-6
    LAMBDA_INIT = 0.8 - 0.6
    NEG_BIG = -1e30
    T = SEQ // P
    KD = D // P
    HT = SEQ // 2
    CH = 4
    CHUNKS = FF // (CH * P)
    QK_COLS = HEADS * 2 * HEAD
    K0, V0 = QK_COLS, 2 * QK_COLS
    X0 = V0 + HEADS * VDIM
    G0 = X0 + GROUPS * P
    HALVES = (slice(0, HT), slice(HT, SEQ))

    x_rows = x.rearrange("b (t p) d -> (b t) p d", p=P)
    y_rows = y.rearrange("b (t p) d -> (b t) p d", p=P)
    w_in_v = w_in.rearrange("l (k p) c -> (l p) k c", p=P)
    up_a_v = w_up_attn.rearrange("l (k p) c -> (l p) k c", p=P)
    up_p_v = w_up_pool.rearrange("l (k p) c -> (l p) k c", p=P)
    w_o_v = w_o.rearrange("l (k p) c -> (l p) k c", p=P)
    mlp_in_v = w_mlp_in.rearrange("l (k p) c -> (l p) k c", p=P)
    mlp_out_v = w_mlp_out.rearrange("l (f p) c -> (l p) f c", p=P)
    pool_w_v = pool_w.rearrange("l g c d -> (l c) g d")

    with ExitStack() as ctx:
        BASE = 1152
        arena_used = []

        def at(name, kb, shape, dt=F32):
            off = BASE + int(kb * KB)
            size = 4
            for n in shape[1:]:
                size *= n
            arena_used.append(off + size)
            return nc.alloc_sbuf_tensor_at(name, shape, dt, offset=off)

        def both(name, kb, shape, apart):
            return (at(name + "_hi", kb, shape, F32R), at(name + "_lo", kb + apart, shape, F32R))

        featT = both("featT", 0, [P, KD, SEQ], 32)
        attnT = both("attnT", 64, [P, HEADS, SEQ], 16)
        h_row = [at(f"h_row{i}", 68 + 4 * i, [P, D]) for i in range(2)]
        g1_row = at("g1_row", 76, [P, D])
        square1 = at("square1", 84, [P, D])
        qT = both("qT", 96, [P, SEQ], 4)
        kT = both("kT", 104, [P, SEQ], 4)
        v_tok = at("v_tok", 112, [P, T, 2, P], F32R)
        wT = [both(f"wT{c}", 120 + 4 * c, [P, 4, P], 2) for c in range(2)]
        xpT = at("xpT", 128, [P, GROUPS, SEQ])
        x_tile = [at(f"x_tile{i}", 128 + 4 * i, [P, D]) for i in range(4)]
        prob = [at(f"prob{c}", 144 + 4 * c, [P, SEQ]) for c in range(2)]
        w_tok = at("w_tok", 152, [P, SEQ])
        qkv = [at(f"qkv{i}", 156 + 1.5 * i, [P, 3 * P]) for i in range(2)]
        qk_norm = [at(f"qk_norm{i}", 208 + i, [P, 2 * P]) for i in range(2)]
        qk_square = at("qk_square", 210, [P, 4, HEAD])
        o_part = at("o_part", 211, [P, P])
        o_sum = [at(f"o_sum{i}", 211.5 + 0.5 * i, [P, P]) for i in range(2)]
        o_square = at("o_square", 212.5, [P, P])
        attn_norm = [at(f"attn_norm{i}", 213 + 0.5 * i, [P, P]) for i in range(2)]
        mixT = both("mixT", 96, [P, GROUPS, SEQ], 16)
        window = [at(f"window{i}", 144 + 4 * i, [P, SEQ]) for i in range(2)]
        pooledT = both("pooledT", 152, [P, SEQ], 4)
        mergedT = at("mergedT", 128, [P, KD, SEQ])
        gate = at("gate", 208, [P, 2, SEQ])
        res = at("res", 64, [P, T, D])
        h2_row = [at(f"h2_row{i}", 144 + 4 * i, [P, D]) for i in range(2)]
        g2_row = at("g2_row", 152, [P, D])
        square2 = at("square2", 156, [P, D])
        uT = (at("uT_hi", 144, [P, CH, SEQ], F32R), at("uT_lo", 96, [P, CH, SEQ], F32R))
        relu = [at(f"relu{i}", 208 + 2 * i, [P, HT]) for i in range(2)]
        u_full = [at(f"u_full{i}", 212 + 2 * i, [P, HT]) for i in range(2)]
        BLOCK = 1024
        raw = [at(f"raw{i}", 192 + 4 * i, [P, BLOCK]) for i in range(4)]
        slot_hi = at("slot_hi", 160, [P, 4, BLOCK], F32R)
        slot_lo = at("slot_lo", 176, [P, 4, BLOCK], F32R)
        more_hi = at("more_hi", 96, [P, 4, BLOCK], F32R)
        more_lo = at("more_lo", 112, [P, 4, BLOCK], F32R)
        in_hi = at("in_hi", 128, [P, 2, BLOCK], F32R)
        in_lo = at("in_lo", 136, [P, 2, BLOCK], F32R)
        slots = [(slot_hi[:, i], slot_lo[:, i]) for i in range(4)]
        slots += [(more_hi[:, i], more_lo[:, i]) for i in range(4)]
        slots += [(in_hi[:, i], in_lo[:, i]) for i in range(2)]
        ident = at("ident", 216, [P, P])
        ident_r = at("ident_r", 216.5, [P, P], F32R)
        mask = at("mask", 217, [P, P])
        mask_r = at("mask_r", 217.5, [P, P], F32R)
        N_ROWS = 2 * D // P + GROUPS + 3
        vec_rows = at("vec_rows", 218, [N_ROWS, P])
        col = at("col", 218.5, [P, N_ROWS])
        lam_in = at("lam_in", 218.75, [P, 4, HEAD])
        lam_prod = at("lam_prod", 219.75, [P, 2, HEAD])
        small = at("small", 220.25, [P, 128])
        BG, PS, SG, QG, KG = 0, 2 * D // P, 2 * D // P + GROUPS, 2 * D // P + GROUPS + 1, 2 * D // P + GROUPS + 2

        def sm(a, n=1):
            return small[:, a:a + n]

        neg_half, lam_sum, lam_exp, neg_lam, k_scale, sub_scale = sm(0, 4), sm(4, 2), sm(6, 2), sm(8), sm(9), sm(10)
        x_ss, x_ms, x_rstd = sm(12, 8), sm(20, 8), sm(28, 8)
        qk_ss = [sm(36 + 4 * i, 4) for i in range(2)]
        qk_ms = sm(44, 4)
        qk_rstd = [sm(48 + 4 * i, 4) for i in range(2)]
        neg_max = [sm(56 + 2 * i, 2) for i in range(2)]
        exp_sum = [sm(60 + 2 * i, 2) for i in range(2)]
        recip = [sm(64 + 2 * i, 2) for i in range(2)]
        coef = sm(68)
        a_ss, a_ms, a_rstd = sm(69), sm(70), sm(71)
        a_scale = [sm(72 + i) for i in range(2)]
        lam_diff = sm(75)
        count_inv = sm(76, 16)
        assert max(arena_used) <= nc.sbuf_usable_end

        bank = ctx.enter_context(nc.psum_tensor("bank", [P, 8, 512], F32))
        PROJ, TA, TB, OUT = 4, 5, 6, 7

        sems = {}

        def sem(name):
            sems[name] = ctx.enter_context(nc.semaphore(name))
            return sems[name]

        passed = sem("passed")
        raw_in = [sem(f"raw_in{i}") for i in range(4)]
        x_in = [sem(f"x_in{i}") for i in range(4)]
        res_in = sem("res_in")
        vec_in, lam_sem, g1_in, g2_in, y_out = sem("vec_in"), sem("lam_sem"), sem("g1_in"), sem("g2_in"), sem("y_out")
        zeroed, const_ready, ident_ready, ident_r_ready, mask_ready = (sem(n) for n in (
            "zeroed", "const_ready", "ident_ready", "ident_r_ready", "mask_ready"))
        vec_full, col_ready, lam_step, lam_exped = (sem(n) for n in ("vec_full", "col_ready", "lam_step", "lam_exped"))
        w_hi, w_ready = sem("w_hi"), sem("w_ready")
        x_squared, x_mean, x_inv, h_ready, xT_full, xT_hi, xT_split = (sem(n) for n in (
            "x_squared", "x_mean", "x_inv", "h_ready", "xT_full", "xT_hi", "xT_split"))
        (proj_full, proj_free, qk_squared, qk_summed, qk_mean, qk_inv, qk_normed, v_hi, v_ready,
         ta_full, ta_hi, ta_free, tb_full, tb_hi, tb_free, score_full, max_ready, exp_ready, recip_ready,
         coef_ready, w_tok_ready, out_full, out_part, out_free, a_squared, a_mean, a_inv, a_scaled,
         a_normed) = (sem(n) for n in (
             "proj_full", "proj_free", "qk_squared", "qk_summed", "qk_mean", "qk_inv", "qk_normed", "v_hi",
             "v_ready", "ta_full", "ta_hi", "ta_free", "tb_full", "tb_hi", "tb_free", "score_full",
             "max_ready", "exp_ready", "recip_ready", "coef_ready", "w_tok_ready", "out_full", "out_part",
             "out_free", "a_squared", "a_mean", "a_inv", "a_scaled", "a_normed"))
        (pool_step, pooled_ready, pooled_hi, pooled_split, mix_full, mix_hi, mix_split, gate_full, gate_ready,
         up_full, gated, merged_ready) = (sem(n) for n in (
             "pool_step", "pooled_ready", "pooled_hi", "pooled_split", "mix_full", "mix_hi", "mix_split",
             "gate_full", "gate_ready", "up_full", "gated", "merged_ready"))
        (m_hi, m_split, wo_full, res_ready, r_squared, r_mean, r_inv, h2_ready, h2T_full, h2T_hi,
         h2T_split) = (sem(n) for n in (
             "m_hi", "m_split", "wo_full", "res_ready", "r_squared", "r_mean", "r_inv", "h2_ready", "h2T_full",
             "h2T_hi", "h2T_split"))
        u_done, relu_ready, u_hi_ready, u_sq_ready, u_split, down_full, y_added = (sem(n) for n in (
            "u_done", "relu_ready", "u_hi_ready", "u_sq_ready", "u_split", "down_full", "y_added"))

        def wait(eng, s, value):
            if not isinstance(value, int) or value > 0:
                eng.wait_ge(s, value)

        def apart(eng):
            eng.sem_inc(passed, 1)

        PIECES = (1, 1, 2)
        POOL_W, WO, MLP0 = 4 * HEADS + 4, 3 * KD + 18, 3 * KD + 26
        MLP_ORDER = [("in", 0), ("in", 1), ("out", 0), ("in", 2), ("out", 1), ("in", 3), ("out", 2), ("out", 3)]
        mlp_pos = {key: i for i, key in enumerate(MLP_ORDER)}

        def tile_block(d, i):
            return 4 * HEADS + 1 + i if isinstance(d, int) and d == 0 else 3 * d + 18 + i

        def k4(ap, n):
            return ap.rearrange("p (k c) -> p k c", k=n)

        def mlp_slot(kind, j):
            return slots[8 + j % 2] if kind == "in" else slots[j]

        block = ctx.enter_context(nc.Block())

        @block.sync
        def _(sp):
            def load(r, src, number, parts=8, behind=4, pieces=1):
                wait(sp, w_ready, number - behind)
                if not isinstance(number, int):
                    apart(sp)
                dst, n = k4(raw[r][:], parts), parts // pieces
                for i in range(pieces):
                    sp.dma_start(dst[:, n * i:n * i + n], src[:, n * i:n * i + n]).then_inc(raw_in[r], 16)

            def load_head(h):
                for i, c0 in enumerate((0, K0, V0)):
                    load(i, w_in_v[:, :, bass.ds(c0 + h * P, P)], 4 * h + 1 + i, pieces=PIECES[i])
                load(3, w_in_v[:, :, bass.ds(X0 + (GROUPS - 1 - h) * P, P)], 4 * h + 4)

            def load_tile(d, behind):
                load(0, w_in_v[:, :, bass.ds(G0 + d * P, P)], tile_block(d, 0), behind=behind)
                load(1, w_in_v[:, :, bass.ds(G0 + D + d * P, P)], tile_block(d, 1), behind=behind)
                sp.wait_ge(w_ready, tile_block(d, 2) - behind)
                apart(sp)
                up = k4(raw[2][:], 8)
                sp.dma_start(up[:, 0:4], up_a_v[:, :, bass.ds(d * P, P)]).then_inc(raw_in[2], 16)
                sp.dma_start(up[:, 4:8], up_p_v[:, :, bass.ds(d * P, P)]).then_inc(raw_in[2], 16)

            def load_chunk(c):
                for i, (kind, j) in enumerate(MLP_ORDER):
                    if kind == "in":
                        load(i % 4, mlp_in_v[:, :, bass.ds((c * CH + j) * P, P)], MLP0 + 8 * c + i)
                    else:
                        load(i % 4, mlp_out_v[:, bass.ds(c * CH + j, 1), :], MLP0 + 8 * c + i, parts=1)

            sp.dma_start(x_tile[0][:], x_rows[0]).then_inc(x_in[0], 16)
            sp.dma_start(g1_row[:], norm1_g.to_broadcast([P, D])).then_inc(g1_in, 16)
            sp.dma_start(x_tile[1][:], x_rows[1]).then_inc(x_in[1], 16)
            for i, c0 in enumerate((0, K0, V0)):
                load(i, w_in_v[:, :, c0:c0 + P], 1 + i, pieces=PIECES[i])
            sp.dma_start(x_tile[2][:], x_rows[2]).then_inc(x_in[2], 16)
            sp.dma_start(x_tile[3][:], x_rows[3]).then_inc(x_in[3], 16)
            for t in range(4, T):
                sp.wait_ge(h_ready, t - 3)
                sp.dma_start(x_tile[t % 4][:], x_rows[t]).then_inc(x_in[t % 4], 16)
            load(3, w_in_v[:, :, X0 + (GROUPS - 1) * P:X0 + GROUPS * P], 4)
            with sp.Fori(1, HEADS) as h:
                load_head(h)
            load_tile(0, 4)
            sp.wait_ge(w_ready, POOL_W - 4)
            sp.dma_start(k4(raw[3][:, 0:GROUPS * P], GROUPS), pool_w_v).then_inc(raw_in[3], 16)
            with sp.Fori(1, KD) as d:
                load_tile(d, 3)
            for b in range(8):
                k = 2 * (b % 4)
                c0 = (b // 4) * 512
                load(b % 4, w_o_v[:, k:k + 2, c0:c0 + 512], WO + b, parts=2, behind=3 if b < 4 else 4,
                     pieces=2 if b == 2 else 1)
            sp.wait_ge(up_full, 4 * KD)
            for t in range(T):
                sp.dma_start(res[:, t, :], x_rows[t]).then_inc(res_in, 16)
            sp.wait_ge(m_split, T)
            sp.dma_start(g2_row[:], norm2_g.to_broadcast([P, D])).then_inc(g2_in, 16)
            load_chunk(0)
            with sp.Fori(1, CHUNKS) as c:
                load_chunk(c)
            for t in range(T):
                sp.wait_ge(y_added, 2 * T * (CHUNKS - 1) + 2 * t + 2)
                sp.dma_start(y_rows[t], res[:, t, :]).then_inc(y_out, 16)
            sp.wait_ge(y_out, 16 * T)

        @block.gpsimd
        def _(pool):
            pool.memset(ident[:], 0.0).then_inc(zeroed, 1)
            pool.memset(mask[:], 0.0).then_inc(zeroed, 1)
            pool.memset(neg_half, -0.5).then_inc(const_ready, 1)
            pool.wait_ge(zeroed, 2)
            pool.affine_select(out=ident[:], in_=ident[:], compare_op=ALU.not_equal, fill=1.0, base=0,
                               pattern=[[-1, P]], channel_multiplier=1).then_inc(ident_ready, 1)
            pool.affine_select(out=mask[:], in_=mask[:], compare_op=ALU.is_ge, fill=NEG_BIG, base=0,
                               pattern=[[-1, P]], channel_multiplier=1).then_inc(mask_ready, 1)
            pool.wait_ge(const_ready, 1)

            def inverse_root(ss, n_mean, ms, out, n, src, src_n, mean_sem, mean_n, inv_sem):
                pool.wait_ge(src, src_n)
                apart(pool)
                pool.tensor_scalar(ms, ss, 1.0 / n_mean, EPS, ALU.mult, ALU.add).then_inc(mean_sem, 1)
                pool.wait_ge(mean_sem, mean_n)
                pool.tensor_tensor(out, ms, neg_half[:, 0:n], ALU.pow).then_inc(inv_sem, 1)

            def x_inverse(t, squared, mean, inv):
                inverse_root(x_ss[:, t:t + 1], D, x_ms[:, t:t + 1], x_rstd[:, t:t + 1], 1, squared, t + 1, mean, t + 1, inv)

            def head(h):
                for s in range(T + 3):
                    if isinstance(h, int) and s < T // 2:
                        for t in (2 * s + 1, 2 * s + 2):
                            if t < T:
                                x_inverse(t, x_squared, x_mean, x_inv)
                    t = s - 3
                    if t >= 0:
                        wait(pool, a_normed, T * h + t - 1)
                        inverse_root(a_ss, VDIM, a_ms, a_rstd, 1, a_squared, T * h + t + 1, a_mean, T * h + t + 1, a_inv)
                        pool.wait_ge(a_inv, T * h + t + 1)
                        pool.tensor_tensor(a_scale[t % 2], a_rstd, recip[t % 2][:, 0:1], ALU.mult).then_inc(a_scaled, 1)
                    if s < T:
                        t = s
                        if t == 0:
                            wait(pool, out_full, T * h)
                        pool.wait_ge(proj_free, (T + 2) * h + t + 1)
                        apart(pool)
                        v = qkv[t % 2][:, 2 * P:3 * P]
                        pool.tensor_copy(v_tok[:, t, 0, :], v).then_inc(v_hi, 1)
                        pool.wait_ge(v_hi, T * h + t + 1)
                        pool.tensor_tensor(v_tok[:, t, 1, :], v, v_tok[:, t, 0, :], ALU.subtract).then_inc(v_ready, 1)
                        wait(pool, qk_normed, T * h + t - 1)
                        inverse_root(qk_ss[t % 2], HEAD, qk_ms, qk_rstd[t % 2], 4,
                                     qk_summed, T * h + t + 1, qk_mean, T * h + t + 1, qk_inv)

            x_inverse(0, x_squared, x_mean, x_inv)
            head(0)
            with pool.Fori(1, HEADS) as h:
                head(h)
            for t in range(T):
                x_inverse(t, r_squared, r_mean, r_inv)

        @block.scalar
        def _(act):
            def split_hi(number, r, loads, slot, used=None, used_n=0, width=BLOCK):
                act.wait_ge(raw_in[r], 16 * loads)
                if used is not None:
                    wait(act, used, used_n)
                nc.scalar.activation(slot[0][:, 0:width], raw[r][:, 0:width], ACT.Copy).then_inc(w_hi, 1)

            rows_of = lambda v: v.rearrange("l (j p) -> (l j) p", p=P)
            act.dma_start(vec_rows[BG:PS, :], rows_of(b_gate)).then_inc(vec_in, 16)
            act.dma_start(vec_rows[PS:SG, :], rows_of(pool_scale)).then_inc(vec_in, 16)
            act.dma_start(vec_rows[SG:SG + 1, :], subln_g).then_inc(vec_in, 16)
            for r, g in ((QG, q_norm_g), (KG, k_norm_g)):
                for c in range(2):
                    act.dma_start(vec_rows[r:r + 1, c * HEAD:(c + 1) * HEAD], g).then_inc(vec_in, 16)
            act.dma_start(lam_in[:].rearrange("p a b -> p (a b)"),
                          lam_params.rearrange("l a b -> l (a b)").to_broadcast([P, 4 * HEAD])).then_inc(lam_sem, 16)

            def x_square(t):
                act.wait_ge(x_in[t % 4], 16 * (t // 4 + 1))
                wait(act, x_squared, t)
                nc.scalar.activation(square1[:], x_tile[t % 4][:], ACT.Square,
                                     accum_out=x_ss[:, t:t + 1]).then_inc(x_squared, 1)

            def x_hi(t):
                for b in range(2):
                    act.wait_ge(xT_full, 2 * t + b + 1)
                    nc.scalar.activation(featT[0][:, 4 * b:4 * b + 4, t * P:(t + 1) * P],
                                         k4(bank[:, 1 + 2 * b, :], 4), ACT.Copy).then_inc(xT_hi, 1)

            def head(h):
                first = isinstance(h, int)
                ta = tb = 0
                for s in range(T + 3):
                    if first and s < T // 2:
                        for t in (2 * s, 2 * s + 1):
                            if t + 2 < T:
                                x_square(t + 2)
                            x_hi(t)
                    t = s - 3
                    if t >= 0:
                        act.wait_ge(out_free, T * h + t + 1)
                        wait(act, a_mean, T * h + t)
                        wait(act, a_squared, T * h + t)
                        nc.scalar.activation(o_square[:], o_sum[t % 2][:], ACT.Square, scale=recip[t % 2][:, 0:1],
                                             accum_out=a_ss).then_inc(a_squared, 1)
                    t = s - 1
                    if 0 <= t < T:
                        act.wait_ge(ta_full, 12 * h + ta + 1)
                        if t == 0:
                            wait(act, score_full, 2 * T * h)
                        if first and t == 0:
                            act.wait_ge(col_ready, 3)
                        sl = slice(t * P, (t + 1) * P)
                        nc.scalar.activation(qT[0][:, sl], bank[:, TA, 0:P], ACT.Copy).then_inc(ta_hi, 1)
                        nc.scalar.activation(kT[0][:, sl], bank[:, TA, P:2 * P], ACT.Copy,
                                             scale=k_scale).then_inc(ta_hi, 1)
                        ta += 1
                    t = s - 2
                    if 0 <= t < T:
                        act.wait_ge(tb_full, 2 * T * h + tb + 1)
                        wait(act, out_full, T * h + t)
                        n = min(t + 1, 4)
                        nc.scalar.activation(wT[0][0][:, 0:n, :], k4(bank[:, TB, 0:n * P], n), ACT.Copy).then_inc(tb_hi, 1)
                        tb += 1
                    if s < T:
                        t = s
                        act.wait_ge(proj_full, (T + 2) * h + t + 1)
                        wait(act, qk_normed, T * h + t - 1)
                        wait(act, v_ready, T * h + t - 1)
                        nc.scalar.activation(qkv[t % 2][:], bank[:, PROJ, 0:3 * P], ACT.Copy).then_inc(proj_free, 1)
                    t = s - 2
                    if 4 <= t < T:
                        act.wait_ge(ta_full, 12 * h + ta + 1)
                        nc.scalar.activation(wT[1][0][:, 0:t - 3, :], k4(bank[:, TA, 0:(t - 3) * P], t - 3),
                                             ACT.Copy).then_inc(ta_hi, 1)
                        ta += 1
                    if s < T:
                        t = s
                        act.wait_ge(proj_free, (T + 2) * h + t + 1)
                        wait(act, qk_summed, T * h + t)
                        nc.scalar.activation(qk_square[:].rearrange("p a b -> p (a b)"), qkv[t % 2][:, 0:2 * P],
                                             ACT.Square).then_inc(qk_squared, 1)
                    else:
                        i = s - T
                        if i < 2:
                            act.wait_ge(proj_full, (T + 2) * h + T + i + 1)
                            apart(act)
                            nc.scalar.activation(xpT[:, bass.ds(GROUPS - 1 - h, 1), i * HT:(i + 1) * HT],
                                                 bank[:, PROJ:PROJ + 1, :], ACT.Copy).then_inc(proj_free, 1)
                    t = s - 1
                    if 0 <= t < T:
                        n = (t + 1) * P
                        wait(act, w_tok_ready, T * h + t)
                        for c in range(2):
                            act.wait_ge(max_ready, 2 * (T * h + t) + c + 1)
                            nc.scalar.activation(prob[c][:, 0:n],
                                                 bank[:, 2 * c:2 * c + 2, :].rearrange("p a b -> p (a b)")[:, 0:n],
                                                 ACT.Exp, bias=neg_max[t % 2][:, c:c + 1],
                                                 accum_out=exp_sum[t % 2][:, c:c + 1]).then_inc(exp_ready, 1)
                    t = s - 2
                    if 0 <= t < T:
                        act.wait_ge(out_full, T * h + t + 1)
                        wait(act, out_free, T * h + t)
                        nc.scalar.activation(o_part[:], bank[:, OUT, P:2 * P], ACT.Copy).then_inc(out_part, 1)
                    t = s - 3
                    if t >= 0:
                        act.wait_ge(tb_full, 2 * T * h + tb + 1)
                        apart(act)
                        nc.scalar.activation(attnT[0][:, bass.ds(h, 1), t * P:(t + 1) * P], bank[:, TB:TB + 1, 0:P],
                                             ACT.Copy, scale=sub_scale).then_inc(tb_hi, 1)
                        tb += 1
                    if s == 2:
                        split_hi(4 * h + 4, 3, h + 1, slots[3], proj_full, (T + 2) * h)
                    if s == T:
                        for i in range(3):
                            split_hi(4 * h + 5 + i, i, PIECES[i] * (h + 2), slots[i], proj_full, (T + 2) * h + T)

            for i in range(3):
                if i == 0:
                    x_square(0)
                    x_square(1)
                split_hi(1 + i, i, PIECES[i], slots[i])
            act.wait_ge(lam_step, 2)
            nc.scalar.activation(lam_exp, lam_sum, ACT.Exp).then_inc(lam_exped, 1)
            head(0)
            with act.Fori(1, HEADS) as h:
                head(h)

            split_hi(POOL_W, 3, HEADS + 1, slots[3], width=GROUPS * P)

            def gates(d, g, i):
                act.wait_ge(gate_full, 4 * d + 2 * g + i + 1)
                wait(act, merged_ready, 2 * d)
                apart(act)
                nc.scalar.activation(gate[:, g, HALVES[i]], bank[:, 2 * g + i, :], ACT.Sigmoid,
                                     bias=col[:, bass.ds(BG + KD * g + d, 1)]).then_inc(gate_ready, 1)

            def next_tile(d, i):
                used = (gate_full, 4 * d + 2 * i + 2) if i < 2 else (up_full, 4 * d + 4)
                split_hi(3 * d + 21 + i, i, PIECES[i] * (HEADS + 2 + d), slots[i], *used)

            def pool_group(g):
                act.wait_ge(pooled_ready, g + 1)
                wait(act, mix_full, 2 * g)
                nc.scalar.activation(pooledT[0][:], window[g % 2][:], ACT.Copy).then_inc(pooled_hi, 1)
                for i, half in enumerate(HALVES):
                    act.wait_ge(mix_full, 2 * g + i + 1)
                    nc.scalar.activation(mixT[0][:, g, half], bank[:, TB + i, :], ACT.Copy,
                                         scale=col[:, PS + g:PS + g + 1]).then_inc(mix_hi, 1)

            gates(0, 0, 0)
            gates(0, 0, 1)
            next_tile(0, 0)
            pool_group(0)
            gates(0, 1, 0)
            pool_group(1)
            gates(0, 1, 1)
            next_tile(0, 1)
            pool_group(2)
            pool_group(3)
            next_tile(0, 2)
            with act.Fori(1, KD) as d:
                for g in range(2):
                    gates(d, g, 0)
                    gates(d, g, 1)
                    next_tile(d, g)
                next_tile(d, 2)

            def merged_hi(t):
                nc.scalar.activation(featT[0][:, :, t * P:(t + 1) * P], mergedT[:, :, t * P:(t + 1) * P],
                                     ACT.Copy).then_inc(m_hi, 1)

            split_hi(WO + 3, 3, HEADS + 2, slots[3], mix_full, 2 * GROUPS)
            act.wait_ge(merged_ready, 2 * KD)
            act.wait_ge(gate_full, 4 * KD)
            merged_hi(0)
            act.wait_ge(up_full, 4 * KD)
            raw_loads = [HEADS + KD + 1, HEADS + KD + 1, PIECES[2] * (HEADS + KD + 1), HEADS + 2]
            for b in range(4):
                split_hi(WO + 4 + b, b, raw_loads[b] + 1, slots[4 + b])
            for t in range(1, T):
                merged_hi(t)

            def chunk_hi(c, kind, j, used, used_n):
                i = mlp_pos[kind, j]
                split_hi(MLP0 + 8 * c + i, i % 4, raw_loads[i % 4] + 2 * c + 2 + i // 4, mlp_slot(kind, j), used, used_n)

            def h2_hi(t):
                for b in range(2):
                    act.wait_ge(h2T_full, 2 * t + b + 1)
                    nc.scalar.activation(featT[0][:, 4 * b:4 * b + 4, t * P:(t + 1) * P],
                                         k4(bank[:, 4 + 2 * (t % 2) + b, :], 4), ACT.Copy).then_inc(h2T_hi, 1)

            for t in range(T):
                act.wait_ge(res_ready, 2 * t + 2)
                wait(act, r_squared, t)
                nc.scalar.activation(square2[:], res[:, t, :], ACT.Square,
                                     accum_out=x_ss[:, t:t + 1]).then_inc(r_squared, 1)
                if t == 2:
                    chunk_hi(0, "in", 0, m_split, T)
                    chunk_hi(0, "in", 1, m_split, T)
                if t:
                    h2_hi(t - 1)

            def up(c):
                first = isinstance(c, int) and c == 0
                for j in range(CH):
                    if j == 0:
                        if first:
                            chunk_hi(c, "out", 0, wo_full, 2 * T)
                        else:
                            chunk_hi(c, "out", 0, down_full, 2 * T * c)
                    for i in range(2):
                        n = 8 * c + 2 * j + i
                        act.wait_ge(u_done, n + 1)
                        wait(act, u_sq_ready, n - 1)
                        nc.scalar.activation(relu[i][:], bank[:, (2 * j + i) % 4, :], ACT.Relu).then_inc(relu_ready, 1)
                        act.wait_ge(relu_ready, n + 1)
                        if first and j == 0 and i == 0:
                            act.wait_ge(h2_ready, T)
                            act.wait_ge(h2T_full, 2 * T)
                        nc.scalar.activation(uT[0][:, j, HALVES[i]], relu[i][:], ACT.Square).then_inc(u_hi_ready, 1)
                    if j == 0:
                        chunk_hi(c, "in", 2, u_done, 8 * c + 2)
                        chunk_hi(c, "out", 1, None, 0)
                    if j == 1:
                        chunk_hi(c, "in", 3, u_done, 8 * c + 4)
                        chunk_hi(c, "out", 2, None, 0)
                    if j == 2:
                        chunk_hi(c, "out", 3, None, 0)

            h2_hi(T - 1)
            up(0)
            with act.Fori(1, CHUNKS) as c:
                chunk_hi(c, "in", 0, u_done, 8 * c - 2)
                chunk_hi(c, "in", 1, u_done, 8 * c)
                up(c)

        @block.vector
        def _(dve):
            def split_lo(number, r, slot, width=BLOCK):
                dve.wait_ge(w_hi, number)
                nc.vector.tensor_tensor(slot[1][:, 0:width], raw[r][:, 0:width], slot[0][:, 0:width],
                                        ALU.subtract).then_inc(w_ready, 1)

            def x_norm(t):
                dve.wait_ge(x_inv, t + 1)
                if t == 0:
                    dve.wait_ge(g1_in, 16)
                wait(dve, xT_full, 2 * (t - 1))
                nc.vector.scalar_tensor_tensor(h_row[t % 2][:], x_tile[t % 4][:], x_rstd[:, t:t + 1], g1_row[:],
                                               ALU.mult, ALU.mult).then_inc(h_ready, 1)

            def x_lo(t):
                for b in range(2):
                    dve.wait_ge(xT_hi, 2 * t + b + 1)
                    dst = (slice(None), slice(4 * b, 4 * b + 4), slice(t * P, (t + 1) * P))
                    nc.vector.tensor_tensor(featT[1][dst], k4(bank[:, 1 + 2 * b, :], 4), featT[0][dst],
                                            ALU.subtract).then_inc(xT_split, 1)

            def head(h):
                first = isinstance(h, int)
                ta = tb = 0
                hi_ta = 0
                for s in range(T + 3):
                    if first and s < T // 2:
                        for t in (2 * s, 2 * s + 1):
                            if t + 1 < T:
                                x_norm(t + 1)
                            x_lo(t)
                    t = s - 2
                    if 0 <= t < T:
                        n = (t + 1) * P
                        dve.wait_ge(exp_ready, 2 * (T * h + t) + 2)
                        nc.vector.reciprocal(recip[t % 2], exp_sum[t % 2]).then_inc(recip_ready, 1)
                        dve.wait_ge(recip_ready, T * h + t + 1)
                        nc.vector.scalar_tensor_tensor(coef, exp_sum[t % 2][:, 0:1], neg_lam, recip[t % 2][:, 1:2],
                                                       ALU.mult, ALU.mult).then_inc(coef_ready, 1)
                        dve.wait_ge(coef_ready, T * h + t + 1)
                        nc.vector.scalar_tensor_tensor(w_tok[:, 0:n], prob[1][:, 0:n], coef, prob[0][:, 0:n],
                                                       ALU.mult, ALU.add).then_inc(w_tok_ready, 1)
                    t = s - 1
                    if 0 <= t < T:
                        dve.wait_ge(qk_inv, T * h + t + 1)
                        nc.vector.tensor_tensor(qk_norm[t % 2][:].rearrange("p (g c) -> p g c", c=HEAD),
                                                qkv[t % 2][:, 0:2 * P].rearrange("p (g c) -> p g c", c=HEAD),
                                                qk_rstd[t % 2].unsqueeze(2).to_broadcast([P, 4, HEAD]),
                                                ALU.mult).then_inc(qk_normed, 1)
                    t = s - 3
                    if t >= 0:
                        dve.wait_ge(a_scaled, T * h + t + 1)
                        nc.vector.tensor_scalar(attn_norm[t % 2][:], o_sum[t % 2][:], a_scale[t % 2], None,
                                                ALU.mult).then_inc(a_normed, 1)
                    t = s - 1
                    if 0 <= t < T:
                        sl = slice(t * P, (t + 1) * P)
                        dve.wait_ge(ta_hi, 20 * h + hi_ta + 2)
                        nc.vector.tensor_tensor(qT[1][:, sl], bank[:, TA, 0:P], qT[0][:, sl], ALU.subtract)
                        nc.vector.scalar_tensor_tensor(kT[1][:, sl], bank[:, TA, P:2 * P], k_scale, kT[0][:, sl],
                                                       ALU.mult, ALU.subtract).then_inc(ta_free, 1)
                        ta += 1
                        hi_ta += 2
                    t = s - 2
                    if 0 <= t < T:
                        n = min(t + 1, 4)
                        dve.wait_ge(tb_hi, 2 * T * h + tb + 1)
                        nc.vector.tensor_tensor(wT[0][1][:, 0:n, :], k4(bank[:, TB, 0:n * P], n), wT[0][0][:, 0:n, :],
                                                ALU.subtract).then_inc(tb_free, 1)
                        tb += 1
                    if 4 <= t < T:
                        dve.wait_ge(ta_hi, 20 * h + hi_ta + 1)
                        nc.vector.tensor_tensor(wT[1][1][:, 0:t - 3, :], k4(bank[:, TA, 0:(t - 3) * P], t - 3),
                                                wT[1][0][:, 0:t - 3, :], ALU.subtract).then_inc(ta_free, 1)
                        ta += 1
                        hi_ta += 1
                    for c in range(2):
                        t = s - 1
                        if 0 <= t < T:
                            n = (t + 1) * P
                            dve.wait_ge(score_full, 2 * (T * h + t) + c + 1)
                            nc.vector.tensor_reduce(neg_max[t % 2][:, c:c + 1],
                                                    bank[:, 2 * c:2 * c + 2, :].rearrange("p a b -> p (a b)")[:, 0:n],
                                                    AX.X, ALU.max, negate=True).then_inc(max_ready, 1)
                        if c == 0 and s < T:
                            dve.wait_ge(qk_squared, T * h + s + 1)
                            nc.vector.tensor_reduce(qk_ss[s % 2], qk_square[:], AX.X, ALU.add).then_inc(qk_summed, 1)
                    t = s - 2
                    if 0 <= t < T:
                        dve.wait_ge(out_part, T * h + t + 1)
                        nc.vector.tensor_tensor(o_sum[t % 2][:], bank[:, OUT, 0:P], o_part[:], ALU.add).then_inc(out_free, 1)
                    t = s - 3
                    if t >= 0:
                        dve.wait_ge(tb_hi, 2 * T * h + tb + 1)
                        nc.vector.scalar_tensor_tensor(attnT[1][:, bass.ds(h, 1), t * P:(t + 1) * P],
                                                       bank[:, TB:TB + 1, 0:P], sub_scale,
                                                       attnT[0][:, bass.ds(h, 1), t * P:(t + 1) * P],
                                                       ALU.mult, ALU.subtract).then_inc(tb_free, 1)
                        tb += 1
                    if s == 2:
                        split_lo(4 * h + 4, 3, slots[3])
                    if s == T:
                        for i in range(3):
                            split_lo(4 * h + 5 + i, i, slots[i])

            dve.wait_ge(ident_ready, 1)
            nc.vector.tensor_copy(ident_r[:], ident[:]).then_inc(ident_r_ready, 1)
            dve.wait_ge(mask_ready, 1)
            nc.vector.tensor_copy(mask_r[:], mask[:]).then_inc(ident_r_ready, 1)
            for i in range(16):
                nc.vector.memset(count_inv[:, i:i + 1], 1.0 / (i + 1))
            dve.wait_ge(lam_sem, 16)
            pairs = lam_in[:].rearrange("p (a b) c -> p a b c", b=2)
            nc.vector.tensor_tensor(lam_prod[:], pairs[:, :, 0, :], pairs[:, :, 1, :], ALU.mult).then_inc(lam_step, 1)
            dve.wait_ge(lam_step, 1)
            nc.vector.tensor_reduce(lam_sum, lam_prod[:], AX.X, ALU.add).then_inc(lam_step, 1)
            x_norm(0)
            for i in range(3):
                split_lo(1 + i, i, slots[i])
            dve.wait_ge(lam_exped, 1)
            nc.vector.tensor_tensor(lam_diff, lam_exp[:, 1:2], lam_exp[:, 0:1], ALU.subtract).then_inc(lam_step, 1)
            dve.wait_ge(lam_step, 3)
            nc.vector.tensor_scalar(neg_lam, lam_diff, -LAMBDA_INIT, None, ALU.add).then_inc(lam_step, 1)
            dve.wait_ge(lam_step, 4)
            dve.wait_ge(vec_full, 1)
            nc.vector.tensor_copy(col[:], bank[:, OUT, 0:N_ROWS]).then_inc(col_ready, 1)
            dve.wait_ge(col_ready, 1)
            nc.vector.scalar_tensor_tensor(k_scale, col[:, QG:QG + 1], float(HEAD) ** -0.5, col[:, KG:KG + 1],
                                           ALU.mult, ALU.mult).then_inc(col_ready, 1)
            nc.vector.tensor_scalar(sub_scale, col[:, SG:SG + 1], 1.0 - LAMBDA_INIT, None, ALU.mult).then_inc(col_ready, 1)
            dve.wait_ge(col_ready, 3)
            head(0)
            with dve.Fori(1, HEADS) as h:
                head(h)

            split_lo(POOL_W, 3, slots[3], width=GROUPS * P)
            step = [0]

            def pool_wait():
                dve.wait_ge(pool_step, step[0])

            def pool_inc(ins):
                step[0] += 1
                ins.then_inc(pool_step, 1)

            def group(g):
                w = 2 << g
                src, into = xpT[:, g, :], (g % 2 + g) % 2
                if g == 0:
                    dve.wait_ge(proj_free, (T + 2) * HEADS)
                for i in range(g + 1):
                    sh = 1 << i
                    dst = window[into]
                    if i == 0 and g > 0:
                        wait(dve, pooled_hi, g)
                    pool_inc(nc.vector.tensor_copy(dst[:, 0:sh], src[:, 0:sh]))
                    pool_inc(nc.vector.tensor_tensor(dst[:, sh:], src[:, sh:], src[:, 0:SEQ - sh], ALU.add))
                    pool_wait()
                    src, into = dst, 1 - into
                assert src is window[g % 2]
                pool_inc(nc.vector.tensor_tensor(src[:, 0:w - 1], src[:, 0:w - 1], count_inv[:, 0:w - 1], ALU.mult))
                pool_inc(nc.vector.tensor_scalar(src[:, w - 1:], src[:, w - 1:], 1.0 / w, None, ALU.mult))
                pool_wait()
                nc.vector.tensor_tensor(src[:], src[:], xpT[:, g, :], ALU.subtract).then_inc(pooled_ready, 1)
                dve.wait_ge(pooled_hi, g + 1)
                nc.vector.tensor_tensor(pooledT[1][:], src[:], pooledT[0][:], ALU.subtract).then_inc(pooled_split, 1)
                for i, half in enumerate(HALVES):
                    dve.wait_ge(mix_hi, 2 * g + i + 1)
                    nc.vector.scalar_tensor_tensor(mixT[1][:, g, half], bank[:, TB + i, :], col[:, PS + g:PS + g + 1],
                                                   mixT[0][:, g, half], ALU.mult, ALU.subtract).then_inc(mix_split, 1)

            def next_tile(d, i):
                split_lo(3 * d + 21 + i, i, slots[i])

            def merge(d):
                for br in range(2):
                    for i, half in enumerate(HALVES):
                        n = 2 * br + i
                        dve.wait_ge(up_full, 4 * d + n + 1)
                        dve.wait_ge(gate_ready, 4 * d + n + 1)
                        nc.vector.tensor_tensor(gate[:, br, half], gate[:, br, half], bank[:, 4 + n, :],
                                                ALU.mult).then_inc(gated, 1)
                        if br == 1:
                            dve.wait_ge(gated, 4 * d + n + 1)
                            nc.vector.tensor_tensor(mergedT[:, bass.ds(d, 1), half], gate[:, 0:1, half],
                                                    gate[:, 1:2, half], ALU.add).then_inc(merged_ready, 1)

            next_tile(0, 0)
            group(0)
            group(1)
            next_tile(0, 1)
            group(2)
            group(3)
            merge(0)
            next_tile(0, 2)
            with dve.Fori(1, KD) as d:
                next_tile(d, 0)
                next_tile(d, 1)
                merge(d)
                next_tile(d, 2)

            def merged_lo(t):
                dst = (slice(None), slice(None), slice(t * P, (t + 1) * P))
                dve.wait_ge(m_hi, t + 1)
                nc.vector.tensor_tensor(featT[1][dst], mergedT[dst], featT[0][dst], ALU.subtract).then_inc(m_split, 1)

            split_lo(WO + 3, 3, slots[3])
            merged_lo(0)
            for b in range(4, 8):
                split_lo(WO + b, b % 4, slots[b])
            for t in range(1, T):
                merged_lo(t)

            def chunk_lo(c, kind, j):
                i = mlp_pos[kind, j]
                split_lo(MLP0 + 8 * c + i, i % 4, mlp_slot(kind, j))

            def h2_lo(t):
                for b in range(2):
                    dve.wait_ge(h2T_hi, 2 * t + b + 1)
                    dst = (slice(None), slice(4 * b, 4 * b + 4), slice(t * P, (t + 1) * P))
                    nc.vector.tensor_tensor(featT[1][dst], k4(bank[:, 4 + 2 * (t % 2) + b, :], 4), featT[0][dst],
                                            ALU.subtract).then_inc(h2T_split, 1)

            dve.wait_ge(res_in, 16 * T)
            for t in range(T):
                for i, half in enumerate(HALVES):
                    n = 2 * t + i
                    dve.wait_ge(wo_full, n + 1)
                    nc.vector.tensor_tensor(res[:, t, half], res[:, t, half], bank[:, n % 4, :],
                                            ALU.add).then_inc(res_ready, 1)
                if t == 2:
                    chunk_lo(0, "in", 0)
                    chunk_lo(0, "in", 1)
                if t:
                    h2_lo(t - 1)
                if t == 0:
                    dve.wait_ge(g2_in, 16)
                dve.wait_ge(r_inv, t + 1)
                dve.wait_ge(res_ready, 2 * t + 2)
                wait(dve, h2T_full, 2 * (t - 1))
                nc.vector.scalar_tensor_tensor(h2_row[t % 2][:], res[:, t, :], x_rstd[:, t:t + 1], g2_row[:],
                                               ALU.mult, ALU.mult).then_inc(h2_ready, 1)

            def up(c):
                for j in range(CH):
                    if j == 0:
                        chunk_lo(c, "out", 0)
                    for i in range(2):
                        n = 8 * c + 2 * j + i
                        dve.wait_ge(relu_ready, n + 1)
                        nc.vector.tensor_tensor(u_full[i][:], relu[i][:], relu[i][:], ALU.mult).then_inc(u_sq_ready, 1)
                        dve.wait_ge(u_sq_ready, n + 1)
                        dve.wait_ge(u_hi_ready, n + 1)
                        nc.vector.tensor_tensor(uT[1][:, j, HALVES[i]], u_full[i][:], uT[0][:, j, HALVES[i]],
                                                ALU.subtract).then_inc(u_split, 1)
                    if j == 0:
                        chunk_lo(c, "in", 2)
                        chunk_lo(c, "out", 1)
                    if j == 1:
                        chunk_lo(c, "in", 3)
                        chunk_lo(c, "out", 2)
                    if j == 2:
                        chunk_lo(c, "out", 3)

            def down(c, between=None):
                for t in range(T):
                    for i, half in enumerate(HALVES):
                        n = 2 * T * c + 2 * t + i
                        dve.wait_ge(down_full, n + 1)
                        nc.vector.tensor_tensor(res[:, t, half], res[:, t, half], bank[:, 4 + (2 * t + i) % 4, :],
                                                ALU.add).then_inc(y_added, 1)
                    if t == 0 and between:
                        between()

            h2_lo(T - 1)
            dve.wait_ge(h2_ready, T)
            up(0)
            with dve.Fori(1, CHUNKS) as c:
                def next_in():
                    chunk_lo(c, "in", 0)
                    chunk_lo(c, "in", 1)
                down(c - 1, next_in)
                up(c)
            down(CHUNKS - 1)

        @block.tensor
        def _(pe):
            def passes(out, pairs, start=True, stop=True):
                steps = [(a, b) for (ah, al), (bh, bl) in pairs for a, b in ((ah, bh), (al, bh), (ah, bl))]
                for i, (a, b) in enumerate(steps):
                    mm = nc.tensor.matmul(out, a, b, start=start and i == 0, stop=stop and i == len(steps) - 1)
                return mm

            def cut(pair, *idx):
                return (pair[0][idx], pair[1][idx])

            ALL = slice(None)

            def wblock(i, n=8):
                return (k4(slots[i][0], n), k4(slots[i][1], n))

            def x_transpose(t):
                pe.wait_ge(h_ready, t + 1)
                for b in range(2):
                    wait(pe, xT_split, 2 * (t - 1) + b + 1)
                    for k in range(4):
                        kk = 4 * b + k
                        mm = nc.tensor.transpose(bank[:, 1 + 2 * b, k * P:(k + 1) * P],
                                                 h_row[t % 2][:, kk * P:(kk + 1) * P], ident[:])
                    mm.then_inc(xT_full, 1)

            def head(h):
                first = isinstance(h, int)
                ta = tb = 0
                ta_of, tb_of = {}, {}

                def project(t, ks):
                    if 0 in ks:
                        if t == 0:
                            pe.wait_ge(w_ready, 4 * h + 3)
                        if first:
                            pe.wait_ge(xT_split, 2 * t + 2)
                        wait(pe, proj_free, (T + 2) * h + t)
                    out = bank[:, PROJ, 0:3 * P].rearrange("p (m c) -> p m c", m=3)
                    for k in ks:
                        a = cut(featT, ALL, k, slice(t * P, (t + 1) * P))
                        b = (slot_hi[:, 0:3, k * P:(k + 1) * P], slot_lo[:, 0:3, k * P:(k + 1) * P])
                        mm = passes(out, [(a, b)], start=k == 0, stop=k == KD - 1)
                    if KD - 1 in ks:
                        mm.then_inc(proj_full, 1)

                def pool_project(i, ks):
                    if 0 in ks:
                        if i == 0:
                            pe.wait_ge(w_ready, 4 * h + 4)
                        pe.wait_ge(proj_free, (T + 2) * h + T + i)
                    w = wblock(3)
                    for k in ks:
                        mm = passes(bank[:, PROJ, :], [(cut(w, ALL, k), cut(featT, ALL, k, HALVES[i]))],
                                    start=k == 0, stop=k == KD - 1)
                    if KD - 1 in ks:
                        mm.then_inc(proj_full, 1)

                def weights_transpose(t, c):
                    n = min(t + 1, 4) if c == 0 else t - 3
                    b = TB if c == 0 else TA
                    for k in range(n):
                        mm = nc.tensor.transpose(bank[:, b, k * P:(k + 1) * P],
                                                 w_tok[:, (4 * c + k) * P:(4 * c + k + 1) * P], ident[:])
                    return mm

                for s in range(T + 3):
                    if first and s < T // 2:
                        for t in (2 * s, 2 * s + 1):
                            x_transpose(t)
                    if s < T:
                        project(s, range(6))
                    elif s == T:
                        pool_project(0, range(8))
                    elif s == T + 1:
                        pool_project(1, range(6))
                    t = s - 1
                    if 0 <= t < T:
                        pe.wait_ge(qk_normed, T * h + t + 1)
                        wait(pe, ta_free, 12 * h + ta)
                        nc.tensor.transpose(bank[:, TA, 0:P], qk_norm[t % 2][:, 0:P], ident[:])
                        nc.tensor.transpose(bank[:, TA, P:2 * P], qk_norm[t % 2][:, P:2 * P],
                                            ident[:]).then_inc(ta_full, 1)
                        ta += 1
                        ta_of["qk", t] = ta
                    t = s - 2
                    if 0 <= t < T:
                        pe.wait_ge(w_tok_ready, T * h + t + 1)
                        wait(pe, tb_free, 2 * T * h + tb)
                        weights_transpose(t, 0).then_inc(tb_full, 1)
                        tb += 1
                        tb_of[t] = tb
                    if s < T:
                        project(s, range(6, 8))
                    if s == T + 1:
                        pool_project(1, range(6, 8))
                    if 4 <= t < T:
                        pe.wait_ge(ta_free, 12 * h + ta)
                        weights_transpose(t, 1).then_inc(ta_full, 1)
                        ta += 1
                        ta_of["w", t] = ta
                    t = s - 1
                    if 0 <= t < T:
                        n = (t + 1) * P
                        pe.wait_ge(ta_free, 12 * h + ta_of["qk", t])
                        if first and t == 4:
                            pe.wait_ge(xT_split, 2 * T)
                        for c in range(2):
                            rows = slice(c * HEAD, (c + 1) * HEAD)
                            wait(pe, exp_ready, 2 * (T * h + t - 1) + c + 1)
                            for p0 in range(0, n, 512):
                                p1 = min(n, p0 + 512)
                                out = bank[:, 2 * c + p0 // 512, 0:p1 - p0]
                                a = cut(qT, rows, slice(t * P, (t + 1) * P))
                                b = cut(kT, rows, slice(p0, p1))
                                diagonal = p1 == n
                                nc.tensor.matmul(out, a[0], b[0], start=True, stop=False)
                                nc.tensor.matmul(out, a[1], b[0], start=False, stop=False)
                                mm = nc.tensor.matmul(out, a[0], b[1], start=False, stop=not diagonal)
                                if diagonal:
                                    mm = nc.tensor.matmul(bank[:, 2 * c + p0 // 512, n - P - p0:n - p0], ident_r[:],
                                                          mask_r[:], start=False, stop=True)
                            mm.then_inc(score_full, 1)
                    t = s - 2
                    if 0 <= t < T:
                        pe.wait_ge(v_ready, T * h + t + 1)
                        wait(pe, out_free, T * h + t)
                        for k in range(t + 1):
                            if k == 0:
                                pe.wait_ge(tb_free, 2 * T * h + tb_of[t])
                            if k == 4:
                                pe.wait_ge(ta_free, 12 * h + ta_of["w", t])
                            hi, lo = (wT[k // 4][i][:, k % 4, :] for i in range(2))
                            wide = (bank[:, OUT, 0:2 * P], hi, v_tok[:, k, :, :].rearrange("p a b -> p (a b)"))
                            narrow = (bank[:, OUT, 0:P], lo, v_tok[:, k, 0, :])
                            for i, m in enumerate((wide, narrow) if k == 0 else (narrow, wide)):
                                mm = nc.tensor.matmul(*m, start=k == 0 and i == 0, stop=k == t and i == 1)
                        mm.then_inc(out_full, 1)
                    t = s - 3
                    if t >= 0:
                        pe.wait_ge(a_normed, T * h + t + 1)
                        pe.wait_ge(tb_free, 2 * T * h + tb)
                        nc.tensor.transpose(bank[:, TB, 0:P], attn_norm[t % 2][:], ident[:]).then_inc(tb_full, 1)
                        tb += 1

            pe.wait_ge(ident_ready, 1)
            pe.wait_ge(ident_r_ready, 2)
            pe.wait_ge(vec_in, 16 * 7)
            nc.tensor.transpose(bank[:, OUT, 0:N_ROWS], vec_rows[:], ident[0:N_ROWS, 0:N_ROWS]).then_inc(vec_full, 1)
            head(0)
            with pe.Fori(1, HEADS) as h:
                head(h)

            def gates(d, g, i):
                pe.wait_ge(w_ready, tile_block(d, g))
                if isinstance(d, int):
                    pe.wait_ge(exp_ready, 2 * T * HEADS)
                else:
                    pe.wait_ge(gate_ready, 4 * (d - 1) + 2 * g + i + 1)
                w = wblock(g)
                passes(bank[:, 2 * g + i, :], [(cut(w, ALL, k), cut(featT, ALL, k, HALVES[i])) for k in range(KD)]
                       ).then_inc(gate_full, 1)

            def up_projections(d):
                pe.wait_ge(w_ready, tile_block(d, 2))
                w = wblock(2)
                for br, src in enumerate((attnT, mixT)):
                    for i in range(2):
                        n = 2 * br + i
                        if not isinstance(d, int):
                            pe.wait_ge(gated, 4 * (d - 1) + n + 1)
                        elif br == 0:
                            pe.wait_ge(proj_free, (T + 2) * HEADS)
                            pe.wait_ge(ta_free, 12 * HEADS)
                            pe.wait_ge(tb_free, 2 * T * HEADS)
                        else:
                            pe.wait_ge(mix_split, 2 * GROUPS)
                        passes(bank[:, 4 + n, :], [(cut(w, ALL, 4 * br + k), cut(src, ALL, k, HALVES[i]))
                                                   for k in range(4)]).then_inc(up_full, 1)

            def pool_map(g):
                w = wblock(3)
                if g == 0:
                    pe.wait_ge(w_ready, POOL_W)
                    pe.wait_ge(tb_free, 2 * T * HEADS)
                    pe.wait_ge(out_free, T * HEADS)
                pe.wait_ge(pooled_split, g + 1)
                for i in range(2):
                    wait(pe, mix_split, 2 * (g - 1) + i + 1)
                    passes(bank[:, TB + i, :], [(cut(w, ALL, g), cut(pooledT, ALL, HALVES[i]))]).then_inc(mix_full, 1)

            gates(0, 0, 0)
            gates(0, 0, 1)
            pool_map(0)
            gates(0, 1, 0)
            pool_map(1)
            gates(0, 1, 1)
            pool_map(2)
            pool_map(3)
            up_projections(0)
            with pe.Fori(1, KD) as d:
                for g in range(2):
                    gates(d, g, 0)
                    gates(d, g, 1)
                up_projections(d)

            def out_projection(t):
                pe.wait_ge(m_split, t + 1)
                for i in range(2):
                    n = 2 * t + i
                    if t == 0:
                        pe.wait_ge(gate_ready, 4 * KD)
                    wait(pe, res_ready, n - 3)
                    pairs = []
                    for k in range(KD):
                        w = (k4(slots[4 * i + k // 2][0], 2), k4(slots[4 * i + k // 2][1], 2))
                        pairs.append((cut(featT, ALL, k, slice(t * P, (t + 1) * P)), cut(w, ALL, k % 2)))
                    pe.wait_ge(w_ready, WO + 4 * i + 3)
                    passes(bank[:, n % 4, :], pairs).then_inc(wo_full, 1)

            def h2_transpose(t):
                pe.wait_ge(h2_ready, t + 1)
                if t < 2:
                    pe.wait_ge(gated, 4 * KD)
                for b in range(2):
                    wait(pe, h2T_split, 2 * (t - 2) + b + 1)
                    for k in range(4):
                        kk = 4 * b + k
                        mm = nc.tensor.transpose(bank[:, 4 + 2 * (t % 2) + b, k * P:(k + 1) * P],
                                                 h2_row[t % 2][:, kk * P:(kk + 1) * P], ident[:])
                    mm.then_inc(h2T_full, 1)

            for t in range(T):
                out_projection(t)
                if t:
                    h2_transpose(t - 1)

            def mlp_up(c):
                first = isinstance(c, int)
                for j in range(CH):
                    pe.wait_ge(w_ready, MLP0 + 8 * c + mlp_pos["in", j])
                    w = tuple(k4(part, 8) for part in mlp_slot("in", j))
                    for i in range(2):
                        n = 2 * j + i
                        if first and n == 0:
                            pe.wait_ge(res_ready, 2 * T)
                            pe.wait_ge(h2T_split, T)
                        if first and n == 1:
                            h2_transpose(T - 1)
                            pe.wait_ge(h2T_split, 2 * T)
                        wait(pe, relu_ready, 8 * c + n - 3)
                        passes(bank[:, n % 4, :], [(cut(w, ALL, k), cut(featT, ALL, k, HALVES[i]))
                                                   for k in range(KD)]).then_inc(u_done, 1)

            def mlp_down(c):
                pe.wait_ge(w_ready, MLP0 + 8 * c + 7)
                for t in range(T):
                    for i, half in enumerate(HALVES):
                        n = 2 * t + i
                        if n == 0:
                            pe.wait_ge(u_split, 8 * c + 4)
                        elif n > 3:
                            pe.wait_ge(y_added, 2 * T * c + n - 3)
                        pairs = [(cut(uT, ALL, j, slice(t * P, (t + 1) * P)),
                                  (slots[j][0][:, half], slots[j][1][:, half])) for j in range(CH)]
                        if t in (0, T // 2) and i == 0:
                            passes(bank[:, 4 + n % 4, :], pairs[:-1], stop=False)
                            pe.wait_ge(u_split, 8 * c + (7 if t == 0 else 8))
                            mm = passes(bank[:, 4 + n % 4, :], pairs[-1:], start=False)
                        else:
                            mm = passes(bank[:, 4 + n % 4, :], pairs)
                        mm.then_inc(down_full, 1)

            mlp_up(0)
            with pe.Fori(1, CHUNKS) as c:
                mlp_down(c - 1)
                mlp_up(c)
            mlp_down(CHUNKS - 1)


_INS = ["x", "norm1_g", "w_in", "b_gate", "q_norm_g", "k_norm_g", "lam_params", "subln_g", "pool_w", "pool_scale",
        "w_up_attn", "w_up_pool", "w_o", "norm2_g", "w_mlp_in", "w_mlp_out"]


def kernel(**inputs):
    import numpy as np
    import concourse.bacc as bacc
    from concourse.bass_utils import run_bass_kernel_spmd

    nc = bacc.Bacc("TRN2", target_bir_lowering=False, num_devices=1, dynamic_dma_scratch_size=1024)
    arrays, args = {}, []
    for name in _INS:
        a = np.ascontiguousarray(inputs[name])
        arrays[f"in_{name}"] = a
        args.append(nc.dram_tensor(f"in_{name}", a.shape, mybir.dt.from_np(a.dtype), kind="ExternalInput").ap())
    args.append(nc.dram_tensor("out_y", inputs["x"].shape, F32, kind="ExternalOutput").ap())
    trunk_layer(nc, *args)
    r = run_bass_kernel_spmd(nc, [arrays], core_ids=[0])
    return r.results[0]["out_y"]
```

```python
from contextlib import ExitStack

import concourse.bass as bass
from concourse import mybir

F32 = mybir.dt.float32
F32R = mybir.dt.float32r
ALU = mybir.AluOpType
ACT = mybir.ActivationFunctionType
AX = mybir.AxisListType

P = 128
KB = 1024


def trunk_layer(nc, x, norm1_g, w_in, b_gate, q_norm_g, k_norm_g, lam_params, subln_g,
                pool_w, pool_scale, w_up_attn, w_up_pool, w_o, norm2_g, w_mlp_in, w_mlp_out, y):
    _, SEQ, D = x.shape
    HEAD = q_norm_g.shape[1]
    VDIM = subln_g.shape[1]
    HEADS = w_up_attn.shape[1] // VDIM
    GROUPS = pool_w.shape[1]
    FF = w_mlp_in.shape[2]
    assert SEQ == D == 1024 and 2 * HEAD == VDIM == P and GROUPS == HEADS == 4
    EPS = 1e-6
    LAMBDA_INIT = 0.8 - 0.6
    NEG_BIG = -1e30
    T = SEQ // P
    KD = D // P
    HT = SEQ // 2
    CH = 4
    CHUNKS = FF // (CH * P)
    QK_COLS = HEADS * 2 * HEAD
    K0, V0 = QK_COLS, 2 * QK_COLS
    X0 = V0 + HEADS * VDIM
    G0 = X0 + GROUPS * P
    HALVES = (slice(0, HT), slice(HT, SEQ))

    x_rows = x.rearrange("b (t p) d -> (b t) p d", p=P)
    y_rows = y.rearrange("b (t p) d -> (b t) p d", p=P)
    w_in_v = w_in.rearrange("l (k p) c -> (l p) k c", p=P)
    up_a_v = w_up_attn.rearrange("l (k p) c -> (l p) k c", p=P)
    up_p_v = w_up_pool.rearrange("l (k p) c -> (l p) k c", p=P)
    w_o_v = w_o.rearrange("l (k p) c -> (l p) k c", p=P)
    mlp_in_v = w_mlp_in.rearrange("l (k p) c -> (l p) k c", p=P)
    mlp_out_v = w_mlp_out.rearrange("l (f p) c -> (l p) f c", p=P)
    pool_w_v = pool_w.rearrange("l g c d -> (l c) g d")

    with ExitStack() as ctx:
        BASE = 1152
        arena_used = []

        def at(name, kb, shape, dt=F32):
            off = BASE + int(kb * KB)
            size = 4
            for n in shape[1:]:
                size *= n
            arena_used.append(off + size)
            return nc.alloc_sbuf_tensor_at(name, shape, dt, offset=off)

        def both(name, kb, shape, apart):
            return (at(name + "_hi", kb, shape, F32R), at(name + "_lo", kb + apart, shape, F32R))

        featT = both("featT", 0, [P, KD, SEQ], 32)
        attnT = both("attnT", 64, [P, HEADS, SEQ], 16)
        h_row = [at(f"h_row{i}", 68 + 4 * i, [P, D]) for i in range(2)]
        g1_row = at("g1_row", 76, [P, D])
        square1 = at("square1", 84, [P, D])
        qT = both("qT", 96, [P, SEQ], 4)
        kT = both("kT", 104, [P, SEQ], 4)
        v_tok = at("v_tok", 112, [P, T, 2, P], F32R)
        wT = [both(f"wT{c}", 120 + 4 * c, [P, 4, P], 2) for c in range(2)]
        xpT = at("xpT", 128, [P, GROUPS, SEQ])
        x_tile = [at(f"x_tile{i}", 128 + 4 * i, [P, D]) for i in range(4)]
        prob = [at(f"prob{c}", 144 + 4 * c, [P, SEQ]) for c in range(2)]
        w_tok = at("w_tok", 152, [P, SEQ])
        qkv = [at(f"qkv{i}", 156 + 1.5 * i, [P, 3 * P]) for i in range(2)]
        qk_norm = [at(f"qk_norm{i}", 208 + i, [P, 2 * P]) for i in range(2)]
        qk_square = at("qk_square", 210, [P, 4, HEAD])
        o_part = at("o_part", 211, [P, P])
        o_sum = [at(f"o_sum{i}", 211.5 + 0.5 * i, [P, P]) for i in range(2)]
        o_square = at("o_square", 212.5, [P, P])
        attn_norm = [at(f"attn_norm{i}", 213 + 0.5 * i, [P, P]) for i in range(2)]
        mixT = both("mixT", 96, [P, GROUPS, SEQ], 16)
        window = [at(f"window{i}", 144 + 4 * i, [P, SEQ]) for i in range(2)]
        pooledT = both("pooledT", 152, [P, SEQ], 4)
        POOL_GROUPS = (3, 2)
        wide_window = {g: [at(f"wide_window{g}_{i}", 96 + 4 * g + 16 * i, [P, SEQ]) for i in range(2)] for g in POOL_GROUPS}
        wide_steps = {3: 0, 2: 8}
        mergedT = at("mergedT", 128, [P, KD, SEQ])
        gate = at("gate", 208, [P, 2, SEQ])
        res = at("res", 64, [P, T, D])
        h2_row = [at(f"h2_row{i}", 144 + 4 * i, [P, D]) for i in range(2)]
        g2_row = at("g2_row", 152, [P, D])
        square2 = at("square2", 156, [P, D])
        uT = (at("uT_hi", 144, [P, CH, SEQ], F32R), at("uT_lo", 96, [P, CH, SEQ], F32R))
        relu = [at(f"relu{i}", 208 + 2 * i, [P, HT]) for i in range(2)]
        u_full = [at(f"u_full{i}", 212 + 2 * i, [P, HT]) for i in range(2)]
        BLOCK = 1024
        raw = [at(f"raw{i}", 192 + 4 * i, [P, BLOCK]) for i in range(4)]
        slot_hi = at("slot_hi", 160, [P, 4, BLOCK], F32R)
        slot_lo = at("slot_lo", 176, [P, 4, BLOCK], F32R)
        more_hi = at("more_hi", 96, [P, 4, BLOCK], F32R)
        more_lo = at("more_lo", 112, [P, 4, BLOCK], F32R)
        in_hi = at("in_hi", 128, [P, 2, BLOCK], F32R)
        in_lo = at("in_lo", 136, [P, 2, BLOCK], F32R)
        slots = [(slot_hi[:, i], slot_lo[:, i]) for i in range(4)]
        slots += [(more_hi[:, i], more_lo[:, i]) for i in range(4)]
        slots += [(in_hi[:, i], in_lo[:, i]) for i in range(2)]
        ident = at("ident", 216, [P, P])
        ident_r = at("ident_r", 216.5, [P, P], F32R)
        mask = at("mask", 217, [P, P])
        mask_r = at("mask_r", 217.5, [P, P], F32R)
        N_ROWS = 2 * D // P + GROUPS + 3
        vec_rows = at("vec_rows", 218, [N_ROWS, P])
        col = at("col", 218.5, [P, N_ROWS])
        lam_in = at("lam_in", 218.75, [P, 4, HEAD])
        lam_prod = at("lam_prod", 219.75, [P, 2, HEAD])
        small = at("small", 220.25, [P, 128])
        BG, PS, SG, QG, KG = 0, 2 * D // P, 2 * D // P + GROUPS, 2 * D // P + GROUPS + 1, 2 * D // P + GROUPS + 2

        def sm(a, n=1):
            return small[:, a:a + n]

        neg_half, lam_sum, lam_exp, neg_lam, k_scale, sub_scale = sm(0, 4), sm(4, 2), sm(6, 2), sm(8), sm(9), sm(10)
        x_ss, x_ms, x_rstd = sm(12, 8), sm(20, 8), sm(28, 8)
        qk_ss = [sm(36 + 4 * i, 4) for i in range(2)]
        qk_ms = sm(44, 4)
        qk_rstd = [sm(48 + 4 * i, 4) for i in range(2)]
        neg_max = [sm(56 + 2 * i, 2) for i in range(2)]
        exp_sum = [sm(60 + 2 * i, 2) for i in range(2)]
        recip = [sm(64 + 2 * i, 2) for i in range(2)]
        coef = sm(68)
        a_ss, a_ms, a_rstd = sm(69), sm(70), sm(71)
        a_scale = [sm(72 + i) for i in range(2)]
        lam_diff = sm(75)
        count_inv = sm(76, 16)
        assert max(arena_used) <= nc.sbuf_usable_end

        bank = ctx.enter_context(nc.psum_tensor("bank", [P, 8, 512], F32))
        PROJ, TA, TB, OUT = 4, 5, 6, 7

        sems = {}

        def sem(name):
            sems[name] = ctx.enter_context(nc.semaphore(name))
            return sems[name]

        passed = sem("passed")
        raw_in = [sem(f"raw_in{i}") for i in range(4)]
        x_in = [sem(f"x_in{i}") for i in range(4)]
        res_in = sem("res_in")
        vec_in, lam_sem, g1_in, g2_in, y_out = sem("vec_in"), sem("lam_sem"), sem("g1_in"), sem("g2_in"), sem("y_out")
        zeroed, const_ready, ident_ready, ident_r_ready, mask_ready = (sem(n) for n in (
            "zeroed", "const_ready", "ident_ready", "ident_r_ready", "mask_ready"))
        vec_full, col_ready, lam_step, lam_exped = (sem(n) for n in ("vec_full", "col_ready", "lam_step", "lam_exped"))
        w_hi, w_ready = sem("w_hi"), sem("w_ready")
        x_squared, x_mean, x_inv, h_ready, xT_full, xT_hi, xT_split = (sem(n) for n in (
            "x_squared", "x_mean", "x_inv", "h_ready", "xT_full", "xT_hi", "xT_split"))
        (proj_full, proj_free, qk_squared, qk_summed, qk_mean, qk_inv, qk_normed, v_hi, v_ready,
         ta_full, ta_hi, ta_free, tb_full, tb_hi, tb_free, score_full, max_ready, exp_ready, recip_ready,
         coef_ready, w_tok_ready, out_full, out_part, out_free, a_squared, a_mean, a_inv, a_scaled,
         a_normed) = (sem(n) for n in (
             "proj_full", "proj_free", "qk_squared", "qk_summed", "qk_mean", "qk_inv", "qk_normed", "v_hi",
             "v_ready", "ta_full", "ta_hi", "ta_free", "tb_full", "tb_hi", "tb_free", "score_full",
             "max_ready", "exp_ready", "recip_ready", "coef_ready", "w_tok_ready", "out_full", "out_part",
             "out_free", "a_squared", "a_mean", "a_inv", "a_scaled", "a_normed"))
        wide_step = sem("wide_step")
        (pool_step, pooled_ready, pooled_hi, pooled_split, mix_full, mix_hi, mix_split, gate_full, gate_ready,
         up_full, gated, merged_ready) = (sem(n) for n in (
             "pool_step", "pooled_ready", "pooled_hi", "pooled_split", "mix_full", "mix_hi", "mix_split",
             "gate_full", "gate_ready", "up_full", "gated", "merged_ready"))
        (m_hi, m_split, wo_full, res_ready, r_squared, r_mean, r_inv, h2_ready, h2T_full, h2T_hi,
         h2T_split) = (sem(n) for n in (
             "m_hi", "m_split", "wo_full", "res_ready", "r_squared", "r_mean", "r_inv", "h2_ready", "h2T_full",
             "h2T_hi", "h2T_split"))
        u_done, relu_ready, u_hi_ready, u_sq_ready, u_split, down_full, y_added = (sem(n) for n in (
            "u_done", "relu_ready", "u_hi_ready", "u_sq_ready", "u_split", "down_full", "y_added"))

        def wait(eng, s, value):
            if not isinstance(value, int) or value > 0:
                eng.wait_ge(s, value)

        def apart(eng):
            eng.sem_inc(passed, 1)

        def steps(h):
            return 3 if isinstance(h, int) and h == HEADS else T

        def lagged(h, s, lag):
            there = s < steps(h) and not (isinstance(h, int) and (s < lag if h == 0 else h == HEADS and s >= lag))
            return there, (s - lag) % T, T * h + s - lag, (h if s >= lag else h - 1)

        def at_head(h, per_head, missing):
            return 0 if isinstance(h, int) and h == 0 else per_head * h - missing

        POOL_STEP = 4
        BANK_USES = T + 2

        def use_of(h, t):
            return BANK_USES * h + t + 1 + (t > POOL_STEP)

        X_TILES = ((1, 2), (3,), (4, 5), (6,), (7,))

        PIECES = (1, 1, 2)
        POOL_W, WO, MLP0 = 4 * HEADS + 4, 3 * KD + 18, 3 * KD + 26
        MLP_ORDER = [("in", 0), ("in", 1), ("out", 0), ("in", 2), ("out", 1), ("in", 3), ("out", 2), ("out", 3)]
        mlp_pos = {key: i for i, key in enumerate(MLP_ORDER)}

        def tile_block(d, i):
            return 4 * HEADS + 1 + i if isinstance(d, int) and d == 0 else 3 * d + 18 + i

        GROUP_ORDER = (0, 1, 3, 2)

        def window_of(g):
            return wide_window[g][g % 2] if g in POOL_GROUPS else window[g % 2]

        def gate_bank(d, g, i):
            return (4, 0, 1, 2)[2 * g + i] if isinstance(d, int) else 2 * g + i

        def up_bank(d, n):
            return (3, 5, 6, 7)[n] if isinstance(d, int) else 4 + n

        def k4(ap, n):
            return ap.rearrange("p (k c) -> p k c", k=n)

        def mlp_slot(kind, j):
            return slots[8 + j % 2] if kind == "in" else slots[j]

        block = ctx.enter_context(nc.Block())

        @block.sync
        def _(sp):
            def load(r, src, number, parts=8, behind=4, pieces=1):
                wait(sp, w_ready, number - behind)
                if not isinstance(number, int):
                    apart(sp)
                dst, n = k4(raw[r][:], parts), parts // pieces
                for i in range(pieces):
                    sp.dma_start(dst[:, n * i:n * i + n], src[:, n * i:n * i + n]).then_inc(raw_in[r], 16)

            def load_head(h):
                for i, c0 in enumerate((0, K0, V0)):
                    load(i, w_in_v[:, :, bass.ds(c0 + h * P, P)], 4 * h + 1 + i, pieces=PIECES[i])
                load(3, w_in_v[:, :, bass.ds(X0 + (GROUPS - 1 - h) * P, P)], 4 * h + 4)

            def load_tile(d, behind):
                load(0, w_in_v[:, :, bass.ds(G0 + d * P, P)], tile_block(d, 0), behind=behind)
                load(1, w_in_v[:, :, bass.ds(G0 + D + d * P, P)], tile_block(d, 1), behind=behind)
                sp.wait_ge(w_ready, tile_block(d, 2) - behind)
                apart(sp)
                up = k4(raw[2][:], 8)
                sp.dma_start(up[:, 0:4], up_a_v[:, :, bass.ds(d * P, P)]).then_inc(raw_in[2], 16)
                sp.dma_start(up[:, 4:8], up_p_v[:, :, bass.ds(d * P, P)]).then_inc(raw_in[2], 16)

            def load_chunk(c):
                for i, (kind, j) in enumerate(MLP_ORDER):
                    if kind == "in":
                        load(i % 4, mlp_in_v[:, :, bass.ds((c * CH + j) * P, P)], MLP0 + 8 * c + i)
                    else:
                        load(i % 4, mlp_out_v[:, bass.ds(c * CH + j, 1), :], MLP0 + 8 * c + i, parts=1)

            sp.dma_start(x_tile[0][:], x_rows[0]).then_inc(x_in[0], 16)
            sp.dma_start(g1_row[:], norm1_g.to_broadcast([P, D])).then_inc(g1_in, 16)
            sp.dma_start(x_tile[1][:], x_rows[1]).then_inc(x_in[1], 16)
            for i, c0 in enumerate((0, K0, V0)):
                load(i, w_in_v[:, :, c0:c0 + P], 1 + i, pieces=PIECES[i])
            sp.dma_start(x_tile[2][:], x_rows[2]).then_inc(x_in[2], 16)
            sp.dma_start(x_tile[3][:], x_rows[3]).then_inc(x_in[3], 16)
            for t in range(4, T):
                sp.wait_ge(h_ready, t - 3)
                sp.dma_start(x_tile[t % 4][:], x_rows[t]).then_inc(x_in[t % 4], 16)
            load(3, w_in_v[:, :, X0 + (GROUPS - 1) * P:X0 + GROUPS * P], 4)
            with sp.Fori(1, HEADS) as h:
                load_head(h)
            load_tile(0, 4)
            sp.wait_ge(w_ready, POOL_W - 4)
            sp.dma_start(k4(raw[3][:, 0:GROUPS * P], GROUPS), pool_w_v).then_inc(raw_in[3], 16)
            with sp.Fori(1, KD) as d:
                load_tile(d, 3)
            for b in range(8):
                k = 2 * (b % 4)
                c0 = (b // 4) * 512
                load(b % 4, w_o_v[:, k:k + 2, c0:c0 + 512], WO + b, parts=2, behind=3 if b < 4 else 4,
                     pieces=2 if b == 2 else 1)
            sp.wait_ge(up_full, 4 * KD)
            for t in range(T):
                sp.dma_start(res[:, t, :], x_rows[t]).then_inc(res_in, 16)
            sp.wait_ge(m_split, T)
            sp.dma_start(g2_row[:], norm2_g.to_broadcast([P, D])).then_inc(g2_in, 16)
            load_chunk(0)
            with sp.Fori(1, CHUNKS) as c:
                load_chunk(c)
            for t in range(T):
                sp.wait_ge(y_added, 2 * T * (CHUNKS - 1) + 2 * t + 2)
                sp.dma_start(y_rows[t], res[:, t, :]).then_inc(y_out, 16)
            sp.wait_ge(y_out, 16 * T)

        @block.gpsimd
        def _(pool):
            pool.memset(ident[:], 0.0).then_inc(zeroed, 1)
            pool.memset(mask[:], 0.0).then_inc(zeroed, 1)
            pool.memset(neg_half, -0.5).then_inc(const_ready, 1)
            pool.wait_ge(zeroed, 2)
            pool.affine_select(out=ident[:], in_=ident[:], compare_op=ALU.not_equal, fill=1.0, base=0,
                               pattern=[[-1, P]], channel_multiplier=1).then_inc(ident_ready, 1)
            pool.affine_select(out=mask[:], in_=mask[:], compare_op=ALU.is_ge, fill=NEG_BIG, base=0,
                               pattern=[[-1, P]], channel_multiplier=1).then_inc(mask_ready, 1)
            pool.wait_ge(const_ready, 1)

            def inverse_root(ss, n_mean, ms, out, n, src, src_n, mean_sem, mean_n, inv_sem):
                pool.wait_ge(src, src_n)
                apart(pool)
                pool.tensor_scalar(ms, ss, 1.0 / n_mean, EPS, ALU.mult, ALU.add).then_inc(mean_sem, 1)
                pool.wait_ge(mean_sem, mean_n)
                pool.tensor_tensor(out, ms, neg_half[:, 0:n], ALU.pow).then_inc(inv_sem, 1)

            def x_inverse(t, squared, mean, inv):
                inverse_root(x_ss[:, t:t + 1], D, x_ms[:, t:t + 1], x_rstd[:, t:t + 1], 1, squared, t + 1, mean, t + 1, inv)

            def output_scale(t, u):
                wait(pool, a_normed, u - 1)
                inverse_root(a_ss, VDIM, a_ms, a_rstd, 1, a_squared, u + 1, a_mean, u + 1, a_inv)
                pool.wait_ge(a_inv, u + 1)
                pool.tensor_tensor(a_scale[t % 2], a_rstd, recip[t % 2][:, 0:1], ALU.mult).then_inc(a_scaled, 1)

            def split_v(h, s):
                there, t, u, of = lagged(h, s, 1)
                if not there:
                    return
                if t == 0:
                    wait(pool, out_full, T * of)
                pool.wait_ge(proj_free, use_of(of, t))
                apart(pool)
                v = qkv[t % 2][:, 2 * P:3 * P]
                pool.tensor_copy(v_tok[:, t, 0, :], v).then_inc(v_hi, 1)
                pool.wait_ge(v_hi, u + 1)
                pool.tensor_tensor(v_tok[:, t, 1, :], v, v_tok[:, t, 0, :], ALU.subtract).then_inc(v_ready, 1)

            def head(h):
                for s in range(steps(h)):
                    if isinstance(h, int) and h == 0 and s < len(X_TILES):
                        for t in X_TILES[s]:
                            if t + 1 < T:
                                x_inverse(t + 1, x_squared, x_mean, x_inv)
                    there, t, u, _ = lagged(h, s, 3)
                    if there:
                        output_scale(t, u)
                    if s == 0:
                        split_v(h, s)
                    there, t, u, _ = lagged(h, s, 0)
                    if there:
                        wait(pool, qk_normed, u - 1)
                        inverse_root(qk_ss[t % 2], HEAD, qk_ms, qk_rstd[t % 2], 4,
                                     qk_summed, u + 1, qk_mean, u + 1, qk_inv)
                    if s > 0:
                        split_v(h, s)

            x_inverse(0, x_squared, x_mean, x_inv)
            x_inverse(1, x_squared, x_mean, x_inv)
            head(0)
            with pool.Fori(1, HEADS) as h:
                head(h)
            head(HEADS)

            for g in POOL_GROUPS:
                here, there = wide_window[g]
                now = xpT[:, g, :]
                for i in range(g + 1):
                    sh = 1 << i
                    if i == 0:
                        pool.wait_ge(score_full, 2 * T * HEADS)
                        pool.wait_ge(out_full, T * HEADS)
                        pool.wait_ge(proj_free, BANK_USES * HEADS)
                    else:
                        pool.wait_ge(wide_step, wide_steps[g] + 2 * i)
                    pool.tensor_copy(here[:, 0:sh], now[:, 0:sh]).then_inc(wide_step, 1)
                    pool.tensor_tensor(here[:, sh:], now[:, sh:], now[:, 0:SEQ - sh], ALU.add).then_inc(wide_step, 1)
                    now, here, there = here, there, here
            for t in range(T):
                x_inverse(t, r_squared, r_mean, r_inv)

        @block.scalar
        def _(act):
            def split_hi(number, r, loads, slot, used=None, used_n=0, width=BLOCK):
                act.wait_ge(raw_in[r], 16 * loads)
                if used is not None:
                    wait(act, used, used_n)
                nc.scalar.activation(slot[0][:, 0:width], raw[r][:, 0:width], ACT.Copy).then_inc(w_hi, 1)

            rows_of = lambda v: v.rearrange("l (j p) -> (l j) p", p=P)
            act.dma_start(vec_rows[BG:PS, :], rows_of(b_gate)).then_inc(vec_in, 16)
            act.dma_start(vec_rows[PS:SG, :], rows_of(pool_scale)).then_inc(vec_in, 16)
            act.dma_start(vec_rows[SG:SG + 1, :], subln_g).then_inc(vec_in, 16)
            for r, g in ((QG, q_norm_g), (KG, k_norm_g)):
                for c in range(2):
                    act.dma_start(vec_rows[r:r + 1, c * HEAD:(c + 1) * HEAD], g).then_inc(vec_in, 16)
            act.dma_start(lam_in[:].rearrange("p a b -> p (a b)"),
                          lam_params.rearrange("l a b -> l (a b)").to_broadcast([P, 4 * HEAD])).then_inc(lam_sem, 16)

            def x_square(t):
                act.wait_ge(x_in[t % 4], 16 * (t // 4 + 1))
                wait(act, x_squared, t)
                nc.scalar.activation(square1[:], x_tile[t % 4][:], ACT.Square,
                                     accum_out=x_ss[:, t:t + 1]).then_inc(x_squared, 1)

            def x_hi(t):
                for b in range(2):
                    act.wait_ge(xT_full, 2 * t + b + 1)
                    nc.scalar.activation(featT[0][:, 4 * b:4 * b + 4, t * P:(t + 1) * P],
                                         k4(bank[:, 1 + 2 * b, :], 4), ACT.Copy).then_inc(xT_hi, 1)

            def take_projection(h, s):
                there, t, u, _ = lagged(h, s, 0)
                if there:
                    act.wait_ge(proj_full, use_of(h, t))
                    wait(act, qk_normed, u - 1)
                    wait(act, v_ready, u - 1)
                    nc.scalar.activation(qkv[t % 2][:], bank[:, PROJ, 0:3 * P], ACT.Copy).then_inc(proj_free, 1)

            def square_qk(h, s):
                there, t, u, _ = lagged(h, s, 0)
                if there:
                    act.wait_ge(proj_free, use_of(h, t))
                    wait(act, qk_summed, u)
                    nc.scalar.activation(qk_square[:].rearrange("p a b -> p (a b)"), qkv[t % 2][:, 0:2 * P],
                                         ACT.Square).then_inc(qk_squared, 1)

            def take_pool(use, g, i):
                act.wait_ge(proj_full, use)
                apart(act)
                nc.scalar.activation(xpT[:, bass.ds(g, 1), i * HT:(i + 1) * HT], bank[:, PROJ:PROJ + 1, :],
                                     ACT.Copy).then_inc(proj_free, 1)

            def head(h):
                first = isinstance(h, int) and h == 0
                ta, ta_parts, tb = at_head(h, 12, 3), at_head(h, 20, 4), at_head(h, 2 * T, 5)
                for s in range(steps(h)):
                    if first and s < len(X_TILES):
                        for t in X_TILES[s]:
                            if t + 2 < T:
                                x_square(t + 2)
                            x_hi(t)
                    there, t, u, _ = lagged(h, s, 3)
                    if there:
                        act.wait_ge(out_free, u + 1)
                        wait(act, a_mean, u)
                        wait(act, a_squared, u)
                        nc.scalar.activation(o_square[:], o_sum[t % 2][:], ACT.Square, scale=recip[t % 2][:, 0:1],
                                             accum_out=a_ss).then_inc(a_squared, 1)
                    there, t, u, _ = lagged(h, s, 1)
                    if there:
                        act.wait_ge(ta_full, ta + 1)
                        if t == 0:
                            wait(act, score_full, 2 * T * h)
                        if first and t == 0:
                            act.wait_ge(col_ready, 3)
                        sl = slice(t * P, (t + 1) * P)
                        nc.scalar.activation(qT[0][:, sl], bank[:, TA, 0:P], ACT.Copy).then_inc(ta_hi, 1)
                        nc.scalar.activation(kT[0][:, sl], bank[:, TA, P:2 * P], ACT.Copy,
                                             scale=k_scale).then_inc(ta_hi, 1)
                        ta = ta + 1
                    there, t, u, _ = lagged(h, s, 2)
                    if there:
                        act.wait_ge(tb_full, tb + 1)
                        wait(act, out_full, u)
                        n = min(t + 1, 4)
                        nc.scalar.activation(wT[0][0][:, 0:n, :], k4(bank[:, TB, 0:n * P], n), ACT.Copy).then_inc(tb_hi, 1)
                        tb = tb + 1
                    if s == 0 and not first:
                        take_pool(BANK_USES * h, GROUPS - h, 1)
                    else:
                        take_projection(h, s)
                    if there and t >= 4:
                        act.wait_ge(ta_full, ta + 1)
                        nc.scalar.activation(wT[1][0][:, 0:t - 3, :], k4(bank[:, TA, 0:(t - 3) * P], t - 3),
                                             ACT.Copy).then_inc(ta_hi, 1)
                        ta = ta + 1
                    if s == 0 and not first:
                        split_hi(4 * h + 3, 2, PIECES[2] * (h + 1), slots[2], proj_full, use_of(h - 1, T - 1))
                    else:
                        square_qk(h, s)
                    there, t, u, _ = lagged(h, s, 1)
                    if there:
                        n = (t + 1) * P
                        wait(act, w_tok_ready, u)
                        for c in range(2):
                            act.wait_ge(max_ready, 2 * u + c + 1)
                            nc.scalar.activation(prob[c][:, 0:n],
                                                 bank[:, 2 * c:2 * c + 2, :].rearrange("p a b -> p (a b)")[:, 0:n],
                                                 ACT.Exp, bias=neg_max[t % 2][:, c:c + 1],
                                                 accum_out=exp_sum[t % 2][:, c:c + 1]).then_inc(exp_ready, 1)
                    if s == POOL_STEP and s < steps(h):
                        if first:
                            act.wait_ge(h_ready, T)
                        take_pool(BANK_USES * h + POOL_STEP + 2, GROUPS - 1 - h, 0)
                    there, t, u, _ = lagged(h, s, 2)
                    if there:
                        act.wait_ge(out_full, u + 1)
                        wait(act, out_free, u)
                        nc.scalar.activation(o_part[:], bank[:, OUT, P:2 * P], ACT.Copy).then_inc(out_part, 1)
                    there, t, u, of = lagged(h, s, 3)
                    if there:
                        act.wait_ge(tb_full, tb + 1)
                        apart(act)
                        nc.scalar.activation(attnT[0][:, bass.ds(of, 1), t * P:(t + 1) * P], bank[:, TB:TB + 1, 0:P],
                                             ACT.Copy, scale=sub_scale).then_inc(tb_hi, 1)
                        tb = tb + 1
                    if s == 0 and not first:
                        take_projection(h, s)
                        square_qk(h, s)
                    if s == 2 and steps(h) == T:
                        split_hi(4 * h + 4, 3, h + 1, slots[3], proj_full, BANK_USES * h)
                    if s == T - 1:
                        for i in range(2):
                            split_hi(4 * h + 5 + i, i, PIECES[i] * (h + 2), slots[i], proj_full, use_of(h, T - 1))

            for i in range(3):
                if i == 0:
                    x_square(0)
                    x_square(1)
                split_hi(1 + i, i, PIECES[i], slots[i])
                if i == 0:
                    x_square(2)
                    x_hi(0)
            act.wait_ge(lam_step, 2)
            nc.scalar.activation(lam_exp, lam_sum, ACT.Exp).then_inc(lam_exped, 1)
            head(0)
            with act.Fori(1, HEADS) as h:
                head(h)

            def gates(d, g, i):
                act.wait_ge(gate_full, 4 * d + 2 * g + i + 1)
                wait(act, merged_ready, 2 * d)
                apart(act)
                nc.scalar.activation(gate[:, g, HALVES[i]], bank[:, gate_bank(d, g, i), :], ACT.Sigmoid,
                                     bias=col[:, bass.ds(BG + KD * g + d, 1)]).then_inc(gate_ready, 1)

            def next_tile(d, i):
                used = (gate_full, 4 * d + 2 * i + 2) if i < 2 else (up_full, 4 * d + 4)
                split_hi(3 * d + 21 + i, i, PIECES[i] * (HEADS + 2 + d), slots[i], *used)

            def pool_group(g):
                n = GROUP_ORDER.index(g)
                act.wait_ge(pooled_ready, n + 1)
                wait(act, mix_full, 2 * n)
                nc.scalar.activation(pooledT[0][:], window_of(g)[:], ACT.Copy).then_inc(pooled_hi, 1)
                for i, half in enumerate(HALVES):
                    act.wait_ge(mix_full, 2 * n + i + 1)
                    nc.scalar.activation(mixT[0][:, g, half], bank[:, TB + i, :], ACT.Copy,
                                         scale=col[:, PS + g:PS + g + 1]).then_inc(mix_hi, 1)

            head(HEADS)
            split_hi(POOL_W, 3, HEADS + 1, slots[3], proj_full, BANK_USES * HEADS, width=GROUPS * P)
            gates(0, 0, 0)
            pool_group(0)
            gates(0, 0, 1)
            next_tile(0, 0)
            pool_group(1)
            gates(0, 1, 0)
            pool_group(3)
            gates(0, 1, 1)
            next_tile(0, 1)
            pool_group(2)
            next_tile(0, 2)
            with act.Fori(1, KD) as d:
                for g in range(2):
                    gates(d, g, 0)
                    gates(d, g, 1)
                    next_tile(d, g)
                next_tile(d, 2)

            def merged_hi(t):
                nc.scalar.activation(featT[0][:, :, t * P:(t + 1) * P], mergedT[:, :, t * P:(t + 1) * P],
                                     ACT.Copy).then_inc(m_hi, 1)

            split_hi(WO + 3, 3, HEADS + 2, slots[3], mix_full, 2 * GROUPS)
            act.wait_ge(merged_ready, 2 * KD)
            act.wait_ge(gate_full, 4 * KD)
            merged_hi(0)
            act.wait_ge(up_full, 4 * KD)
            raw_loads = [HEADS + KD + 1, HEADS + KD + 1, PIECES[2] * (HEADS + KD + 1), HEADS + 2]
            for b in range(4):
                split_hi(WO + 4 + b, b, raw_loads[b] + 1, slots[4 + b])
            for t in range(1, T):
                merged_hi(t)

            def chunk_hi(c, kind, j, used, used_n):
                i = mlp_pos[kind, j]
                split_hi(MLP0 + 8 * c + i, i % 4, raw_loads[i % 4] + 2 * c + 2 + i // 4, mlp_slot(kind, j), used, used_n)

            def h2_hi(t):
                for b in range(2):
                    act.wait_ge(h2T_full, 2 * t + b + 1)
                    nc.scalar.activation(featT[0][:, 4 * b:4 * b + 4, t * P:(t + 1) * P],
                                         k4(bank[:, 4 + 2 * (t % 2) + b, :], 4), ACT.Copy).then_inc(h2T_hi, 1)

            for t in range(T):
                act.wait_ge(res_ready, 2 * t + 2)
                wait(act, r_squared, t)
                nc.scalar.activation(square2[:], res[:, t, :], ACT.Square,
                                     accum_out=x_ss[:, t:t + 1]).then_inc(r_squared, 1)
                if t == 2:
                    chunk_hi(0, "in", 0, m_split, T)
                    chunk_hi(0, "in", 1, m_split, T)
                if t:
                    h2_hi(t - 1)

            def up(c):
                first = isinstance(c, int) and c == 0
                for j in range(CH):
                    if j == 0:
                        if first:
                            chunk_hi(c, "out", 0, wo_full, 2 * T)
                        else:
                            chunk_hi(c, "out", 0, down_full, 2 * T * c)
                    for i in range(2):
                        n = 8 * c + 2 * j + i
                        act.wait_ge(u_done, n + 1)
                        wait(act, u_sq_ready, n - 1)
                        nc.scalar.activation(relu[i][:], bank[:, (2 * j + i) % 4, :], ACT.Relu).then_inc(relu_ready, 1)
                        act.wait_ge(relu_ready, n + 1)
                        if first and j == 0 and i == 0:
                            act.wait_ge(h2_ready, T)
                            act.wait_ge(h2T_full, 2 * T)
                        nc.scalar.activation(uT[0][:, j, HALVES[i]], relu[i][:], ACT.Square).then_inc(u_hi_ready, 1)
                    if j == 0:
                        chunk_hi(c, "in", 2, u_done, 8 * c + 2)
                        chunk_hi(c, "out", 1, None, 0)
                    if j == 1:
                        chunk_hi(c, "in", 3, u_done, 8 * c + 4)
                        chunk_hi(c, "out", 2, None, 0)
                    if j == 2:
                        chunk_hi(c, "out", 3, None, 0)

            h2_hi(T - 1)
            up(0)
            with act.Fori(1, CHUNKS) as c:
                chunk_hi(c, "in", 0, u_done, 8 * c - 2)
                chunk_hi(c, "in", 1, u_done, 8 * c)
                up(c)

        @block.vector
        def _(dve):
            def split_lo(number, r, slot, width=BLOCK):
                dve.wait_ge(w_hi, number)
                nc.vector.tensor_tensor(slot[1][:, 0:width], raw[r][:, 0:width], slot[0][:, 0:width],
                                        ALU.subtract).then_inc(w_ready, 1)

            def x_norm(t):
                dve.wait_ge(x_inv, t + 1)
                if t == 0:
                    dve.wait_ge(g1_in, 16)
                wait(dve, xT_full, 2 * (t - 1))
                nc.vector.scalar_tensor_tensor(h_row[t % 2][:], x_tile[t % 4][:], x_rstd[:, t:t + 1], g1_row[:],
                                               ALU.mult, ALU.mult).then_inc(h_ready, 1)

            def x_lo(t):
                for b in range(2):
                    dve.wait_ge(xT_hi, 2 * t + b + 1)
                    dst = (slice(None), slice(4 * b, 4 * b + 4), slice(t * P, (t + 1) * P))
                    nc.vector.tensor_tensor(featT[1][dst], k4(bank[:, 1 + 2 * b, :], 4), featT[0][dst],
                                            ALU.subtract).then_inc(xT_split, 1)

            def sum_squares(h, s):
                there, t, u, _ = lagged(h, s, 0)
                if there:
                    dve.wait_ge(qk_squared, u + 1)
                    nc.vector.tensor_reduce(qk_ss[t % 2], qk_square[:], AX.X, ALU.add).then_inc(qk_summed, 1)

            def head(h):
                first = isinstance(h, int) and h == 0
                ta_parts, tb = at_head(h, 20, 4), at_head(h, 2 * T, 5)
                for s in range(steps(h)):
                    if first and s < len(X_TILES):
                        for t in X_TILES[s]:
                            if t + 1 < T:
                                x_norm(t + 1)
                            x_lo(t)
                    there, t, u, _ = lagged(h, s, 2)
                    if there:
                        n = (t + 1) * P
                        dve.wait_ge(exp_ready, 2 * u + 2)
                        nc.vector.reciprocal(recip[t % 2], exp_sum[t % 2]).then_inc(recip_ready, 1)
                        dve.wait_ge(recip_ready, u + 1)
                        nc.vector.scalar_tensor_tensor(coef, exp_sum[t % 2][:, 0:1], neg_lam, recip[t % 2][:, 1:2],
                                                       ALU.mult, ALU.mult).then_inc(coef_ready, 1)
                        dve.wait_ge(coef_ready, u + 1)
                        nc.vector.scalar_tensor_tensor(w_tok[:, 0:n], prob[1][:, 0:n], coef, prob[0][:, 0:n],
                                                       ALU.mult, ALU.add).then_inc(w_tok_ready, 1)
                    there, t, u, _ = lagged(h, s, 1)
                    if there:
                        dve.wait_ge(qk_inv, u + 1)
                        nc.vector.tensor_tensor(qk_norm[t % 2][:].rearrange("p (g c) -> p g c", c=HEAD),
                                                qkv[t % 2][:, 0:2 * P].rearrange("p (g c) -> p g c", c=HEAD),
                                                qk_rstd[t % 2].unsqueeze(2).to_broadcast([P, 4, HEAD]),
                                                ALU.mult).then_inc(qk_normed, 1)
                    there, t, u, _ = lagged(h, s, 3)
                    if there:
                        dve.wait_ge(a_scaled, u + 1)
                        nc.vector.tensor_scalar(attn_norm[t % 2][:], o_sum[t % 2][:], a_scale[t % 2], None,
                                                ALU.mult).then_inc(a_normed, 1)
                    there, t, u, _ = lagged(h, s, 1)
                    if there:
                        sl = slice(t * P, (t + 1) * P)
                        dve.wait_ge(ta_hi, ta_parts + 2)
                        nc.vector.tensor_tensor(qT[1][:, sl], bank[:, TA, 0:P], qT[0][:, sl], ALU.subtract)
                        nc.vector.scalar_tensor_tensor(kT[1][:, sl], bank[:, TA, P:2 * P], k_scale, kT[0][:, sl],
                                                       ALU.mult, ALU.subtract).then_inc(ta_free, 1)
                        ta_parts = ta_parts + 2
                    there, t, u, _ = lagged(h, s, 2)
                    if there:
                        n = min(t + 1, 4)
                        dve.wait_ge(tb_hi, tb + 1)
                        nc.vector.tensor_tensor(wT[0][1][:, 0:n, :], k4(bank[:, TB, 0:n * P], n), wT[0][0][:, 0:n, :],
                                                ALU.subtract).then_inc(tb_free, 1)
                        tb = tb + 1
                    if there and t >= 4:
                        dve.wait_ge(ta_hi, ta_parts + 1)
                        nc.vector.tensor_tensor(wT[1][1][:, 0:t - 3, :], k4(bank[:, TA, 0:(t - 3) * P], t - 3),
                                                wT[1][0][:, 0:t - 3, :], ALU.subtract).then_inc(ta_free, 1)
                        ta_parts = ta_parts + 1
                    if s == 0 and not first:
                        split_lo(4 * h + 3, 2, slots[2])
                    there, t, u, _ = lagged(h, s, 1)
                    for c in range(2):
                        if there:
                            n = (t + 1) * P
                            dve.wait_ge(score_full, 2 * u + c + 1)
                            nc.vector.tensor_reduce(neg_max[t % 2][:, c:c + 1],
                                                    bank[:, 2 * c:2 * c + 2, :].rearrange("p a b -> p (a b)")[:, 0:n],
                                                    AX.X, ALU.max, negate=True).then_inc(max_ready, 1)
                        if c == 0 and (first or s > 0):
                            sum_squares(h, s)
                    there, t, u, _ = lagged(h, s, 2)
                    if there:
                        dve.wait_ge(out_part, u + 1)
                        nc.vector.tensor_tensor(o_sum[t % 2][:], bank[:, OUT, 0:P], o_part[:], ALU.add).then_inc(out_free, 1)
                    there, t, u, of = lagged(h, s, 3)
                    if there:
                        dve.wait_ge(tb_hi, tb + 1)
                        nc.vector.scalar_tensor_tensor(attnT[1][:, bass.ds(of, 1), t * P:(t + 1) * P],
                                                       bank[:, TB:TB + 1, 0:P], sub_scale,
                                                       attnT[0][:, bass.ds(of, 1), t * P:(t + 1) * P],
                                                       ALU.mult, ALU.subtract).then_inc(tb_free, 1)
                        tb = tb + 1
                    if s == 0 and not first:
                        sum_squares(h, s)
                    if s == 2 and steps(h) == T:
                        split_lo(4 * h + 4, 3, slots[3])
                    if s == T - 1:
                        for i in range(2):
                            split_lo(4 * h + 5 + i, i, slots[i])

            dve.wait_ge(ident_ready, 1)
            nc.vector.tensor_copy(ident_r[:], ident[:]).then_inc(ident_r_ready, 1)
            dve.wait_ge(mask_ready, 1)
            nc.vector.tensor_copy(mask_r[:], mask[:]).then_inc(ident_r_ready, 1)
            for i in range(16):
                nc.vector.memset(count_inv[:, i:i + 1], 1.0 / (i + 1))
            dve.wait_ge(lam_sem, 16)
            pairs = lam_in[:].rearrange("p (a b) c -> p a b c", b=2)
            nc.vector.tensor_tensor(lam_prod[:], pairs[:, :, 0, :], pairs[:, :, 1, :], ALU.mult).then_inc(lam_step, 1)
            dve.wait_ge(lam_step, 1)
            nc.vector.tensor_reduce(lam_sum, lam_prod[:], AX.X, ALU.add).then_inc(lam_step, 1)
            x_norm(0)
            split_lo(1, 0, slots[0])
            x_norm(1)
            x_lo(0)
            for i in (1, 2):
                split_lo(1 + i, i, slots[i])
            dve.wait_ge(lam_exped, 1)
            nc.vector.tensor_tensor(lam_diff, lam_exp[:, 1:2], lam_exp[:, 0:1], ALU.subtract).then_inc(lam_step, 1)
            dve.wait_ge(lam_step, 3)
            nc.vector.tensor_scalar(neg_lam, lam_diff, -LAMBDA_INIT, None, ALU.add).then_inc(lam_step, 1)
            dve.wait_ge(lam_step, 4)
            dve.wait_ge(vec_full, 1)
            nc.vector.tensor_copy(col[:], bank[:, OUT, 0:N_ROWS]).then_inc(col_ready, 1)
            dve.wait_ge(col_ready, 1)
            nc.vector.scalar_tensor_tensor(k_scale, col[:, QG:QG + 1], float(HEAD) ** -0.5, col[:, KG:KG + 1],
                                           ALU.mult, ALU.mult).then_inc(col_ready, 1)
            nc.vector.tensor_scalar(sub_scale, col[:, SG:SG + 1], 1.0 - LAMBDA_INIT, None, ALU.mult).then_inc(col_ready, 1)
            dve.wait_ge(col_ready, 3)
            head(0)
            with dve.Fori(1, HEADS) as h:
                head(h)
            head(HEADS)

            split_lo(POOL_W, 3, slots[3], width=GROUPS * P)
            step = [0]

            def pool_wait():
                dve.wait_ge(pool_step, step[0])

            def pool_inc(ins):
                step[0] += 1
                ins.then_inc(pool_step, 1)

            def sums(g):
                src, into = xpT[:, g, :], 0
                if g == 0:
                    dve.wait_ge(proj_free, BANK_USES * HEADS)
                for i in range(g + 1):
                    sh = 1 << i
                    dst = window[into]
                    if i == 0:
                        wait(dve, pooled_hi, g)
                    pool_inc(nc.vector.tensor_copy(dst[:, 0:sh], src[:, 0:sh]))
                    pool_inc(nc.vector.tensor_tensor(dst[:, sh:], src[:, sh:], src[:, 0:SEQ - sh], ALU.add))
                    pool_wait()
                    src, into = dst, 1 - into

            def group(g):
                w = 2 << g
                n = GROUP_ORDER.index(g)
                src = window_of(g)
                if g in POOL_GROUPS:
                    dve.wait_ge(wide_step, wide_steps[g] + 2 * g + 2)
                else:
                    sums(g)
                pool_inc(nc.vector.tensor_tensor(src[:, 0:w - 1], src[:, 0:w - 1], count_inv[:, 0:w - 1], ALU.mult))
                pool_wait()
                nc.vector.tensor_tensor(src[:, 0:w - 1], src[:, 0:w - 1], xpT[:, g, 0:w - 1], ALU.subtract)
                nc.vector.scalar_tensor_tensor(src[:, w - 1:], src[:, w - 1:], 1.0 / w, xpT[:, g, w - 1:],
                                               ALU.mult, ALU.subtract).then_inc(pooled_ready, 1)
                dve.wait_ge(pooled_ready, n + 1)
                dve.wait_ge(pooled_hi, n + 1)
                nc.vector.tensor_tensor(pooledT[1][:], src[:], pooledT[0][:], ALU.subtract).then_inc(pooled_split, 1)
                for i, half in enumerate(HALVES):
                    dve.wait_ge(mix_hi, 2 * n + i + 1)
                    nc.vector.scalar_tensor_tensor(mixT[1][:, g, half], bank[:, TB + i, :], col[:, PS + g:PS + g + 1],
                                                   mixT[0][:, g, half], ALU.mult, ALU.subtract).then_inc(mix_split, 1)

            def next_tile(d, i):
                split_lo(3 * d + 21 + i, i, slots[i])

            def merge(d):
                for br in range(2):
                    for i, half in enumerate(HALVES):
                        n = 2 * br + i
                        dve.wait_ge(up_full, 4 * d + n + 1)
                        dve.wait_ge(gate_ready, 4 * d + n + 1)
                        nc.vector.tensor_tensor(gate[:, br, half], gate[:, br, half], bank[:, up_bank(d, n), :],
                                                ALU.mult).then_inc(gated, 1)
                        if br == 1:
                            dve.wait_ge(gated, 4 * d + n + 1)
                            nc.vector.tensor_tensor(mergedT[:, bass.ds(d, 1), half], gate[:, 0:1, half],
                                                    gate[:, 1:2, half], ALU.add).then_inc(merged_ready, 1)

            group(0)
            next_tile(0, 0)
            group(1)
            group(3)
            next_tile(0, 1)
            group(2)
            merge(0)
            next_tile(0, 2)
            with dve.Fori(1, KD) as d:
                next_tile(d, 0)
                next_tile(d, 1)
                merge(d)
                next_tile(d, 2)

            def merged_lo(t):
                dst = (slice(None), slice(None), slice(t * P, (t + 1) * P))
                dve.wait_ge(m_hi, t + 1)
                nc.vector.tensor_tensor(featT[1][dst], mergedT[dst], featT[0][dst], ALU.subtract).then_inc(m_split, 1)

            split_lo(WO + 3, 3, slots[3])
            merged_lo(0)
            for b in range(4, 8):
                split_lo(WO + b, b % 4, slots[b])
            for t in range(1, T):
                merged_lo(t)

            def chunk_lo(c, kind, j):
                i = mlp_pos[kind, j]
                split_lo(MLP0 + 8 * c + i, i % 4, mlp_slot(kind, j))

            def h2_lo(t):
                for b in range(2):
                    dve.wait_ge(h2T_hi, 2 * t + b + 1)
                    dst = (slice(None), slice(4 * b, 4 * b + 4), slice(t * P, (t + 1) * P))
                    nc.vector.tensor_tensor(featT[1][dst], k4(bank[:, 4 + 2 * (t % 2) + b, :], 4), featT[0][dst],
                                            ALU.subtract).then_inc(h2T_split, 1)

            dve.wait_ge(res_in, 16 * T)
            for t in range(T):
                for i, half in enumerate(HALVES):
                    n = 2 * t + i
                    dve.wait_ge(wo_full, n + 1)
                    nc.vector.tensor_tensor(res[:, t, half], res[:, t, half], bank[:, n % 4, :],
                                            ALU.add).then_inc(res_ready, 1)
                if t == 2:
                    chunk_lo(0, "in", 0)
                    chunk_lo(0, "in", 1)
                if t:
                    h2_lo(t - 1)
                if t == 0:
                    dve.wait_ge(g2_in, 16)
                dve.wait_ge(r_inv, t + 1)
                dve.wait_ge(res_ready, 2 * t + 2)
                wait(dve, h2T_full, 2 * (t - 1))
                nc.vector.scalar_tensor_tensor(h2_row[t % 2][:], res[:, t, :], x_rstd[:, t:t + 1], g2_row[:],
                                               ALU.mult, ALU.mult).then_inc(h2_ready, 1)

            def up(c):
                for j in range(CH):
                    if j == 0:
                        chunk_lo(c, "out", 0)
                    for i in range(2):
                        n = 8 * c + 2 * j + i
                        dve.wait_ge(relu_ready, n + 1)
                        nc.vector.tensor_tensor(u_full[i][:], relu[i][:], relu[i][:], ALU.mult).then_inc(u_sq_ready, 1)
                        dve.wait_ge(u_sq_ready, n + 1)
                        dve.wait_ge(u_hi_ready, n + 1)
                        nc.vector.tensor_tensor(uT[1][:, j, HALVES[i]], u_full[i][:], uT[0][:, j, HALVES[i]],
                                                ALU.subtract).then_inc(u_split, 1)
                    if j == 0:
                        chunk_lo(c, "in", 2)
                        chunk_lo(c, "out", 1)
                    if j == 1:
                        chunk_lo(c, "in", 3)
                        chunk_lo(c, "out", 2)
                    if j == 2:
                        chunk_lo(c, "out", 3)

            def down(c, between=None):
                for t in range(T):
                    for i, half in enumerate(HALVES):
                        n = 2 * T * c + 2 * t + i
                        dve.wait_ge(down_full, n + 1)
                        nc.vector.tensor_tensor(res[:, t, half], res[:, t, half], bank[:, 4 + (2 * t + i) % 4, :],
                                                ALU.add).then_inc(y_added, 1)
                    if t == 0 and between:
                        between()

            h2_lo(T - 1)
            dve.wait_ge(h2_ready, T)
            up(0)
            with dve.Fori(1, CHUNKS) as c:
                def next_in():
                    chunk_lo(c, "in", 0)
                    chunk_lo(c, "in", 1)
                down(c - 1, next_in)
                up(c)
            down(CHUNKS - 1)

        @block.tensor
        def _(pe):
            def passes(out, pairs, start=True, stop=True):
                steps = [(a, b) for (ah, al), (bh, bl) in pairs for a, b in ((ah, bh), (al, bh), (ah, bl))]
                for i, (a, b) in enumerate(steps):
                    mm = nc.tensor.matmul(out, a, b, start=start and i == 0, stop=stop and i == len(steps) - 1)
                return mm

            def cut(pair, *idx):
                return (pair[0][idx], pair[1][idx])

            ALL = slice(None)

            def wblock(i, n=8):
                return (k4(slots[i][0], n), k4(slots[i][1], n))

            def x_transpose(t):
                pe.wait_ge(h_ready, t + 1)
                for b in range(2):
                    wait(pe, xT_split, 2 * (t - 1) + b + 1)
                    for k in range(4):
                        kk = 4 * b + k
                        mm = nc.tensor.transpose(bank[:, 1 + 2 * b, k * P:(k + 1) * P],
                                                 h_row[t % 2][:, kk * P:(kk + 1) * P], ident[:])
                    mm.then_inc(xT_full, 1)

            def project(h, t, ks):
                first = isinstance(h, int)
                if 0 in ks:
                    if t == 0:
                        pe.wait_ge(w_ready, 4 * h + 3)
                    if first:
                        pe.wait_ge(xT_split, 2 * t + 2)
                    wait(pe, proj_free, use_of(h, t) - 1)
                out = bank[:, PROJ, 0:3 * P].rearrange("p (m c) -> p m c", m=3)
                for k in ks:
                    a = cut(featT, ALL, k, slice(t * P, (t + 1) * P))
                    b = (slot_hi[:, 0:3, k * P:(k + 1) * P], slot_lo[:, 0:3, k * P:(k + 1) * P])
                    mm = passes(out, [(a, b)], start=k == 0, stop=k == KD - 1)
                if KD - 1 in ks:
                    mm.then_inc(proj_full, 1)

            def pool_project(h, i, ks):
                if 0 in ks:
                    pe.wait_ge(w_ready, 4 * h + 4)
                    pe.wait_ge(proj_free, BANK_USES * h + (POOL_STEP + 1 if i == 0 else BANK_USES - 1))
                w = wblock(3)
                for k in ks:
                    mm = passes(bank[:, PROJ, :], [(cut(w, ALL, k), cut(featT, ALL, k, HALVES[i]))],
                                start=k == 0, stop=k == KD - 1)
                if KD - 1 in ks:
                    mm.then_inc(proj_full, 1)

            def weights_transpose(t, c):
                n = min(t + 1, 4) if c == 0 else t - 3
                b = TB if c == 0 else TA
                for k in range(n):
                    mm = nc.tensor.transpose(bank[:, b, k * P:(k + 1) * P],
                                             w_tok[:, (4 * c + k) * P:(4 * c + k + 1) * P], ident[:])
                return mm

            def head(h, between=None):
                first = isinstance(h, int) and h == 0
                ta, tb = at_head(h, 12, 3), at_head(h, 2 * T, 5)
                for s in range(steps(h)):
                    x_tiles = X_TILES[s] if first and s < len(X_TILES) else ()
                    for t in x_tiles[:-1]:
                        x_transpose(t)
                    projects = lagged(h, s, 0)[0]
                    if s == 0 and not first:
                        pool_project(h - 1, 1, range(6))
                    elif projects:
                        project(h, s, range(6))
                    for t in x_tiles[-1:]:
                        x_transpose(t)
                    there, t, u, _ = lagged(h, s, 1)
                    if there:
                        pe.wait_ge(qk_normed, u + 1)
                        wait(pe, ta_free, ta)
                        nc.tensor.transpose(bank[:, TA, 0:P], qk_norm[t % 2][:, 0:P], ident[:])
                        nc.tensor.transpose(bank[:, TA, P:2 * P], qk_norm[t % 2][:, P:2 * P],
                                            ident[:]).then_inc(ta_full, 1)
                        ta = ta + 1
                    there, t, u, _ = lagged(h, s, 2)
                    if there:
                        pe.wait_ge(w_tok_ready, u + 1)
                        wait(pe, tb_free, tb)
                        weights_transpose(t, 0).then_inc(tb_full, 1)
                        tb = tb + 1
                    if s == 0 and not first:
                        pool_project(h - 1, 1, range(6, 8))
                    elif projects:
                        project(h, s, range(6, 8))
                    qk_use = ta
                    if there and t >= 4:
                        wait(pe, ta_free, ta)
                        weights_transpose(t, 1).then_inc(ta_full, 1)
                        ta = ta + 1
                    there, t, u, _ = lagged(h, s, 1)
                    if there:
                        n = (t + 1) * P
                        pe.wait_ge(ta_free, qk_use)
                        if first and t == 4:
                            pe.wait_ge(xT_split, 2 * T)
                        for c in range(2):
                            rows = slice(c * HEAD, (c + 1) * HEAD)
                            wait(pe, exp_ready, 2 * (u - 1) + c + 1)
                            for p0 in range(0, n, 512):
                                p1 = min(n, p0 + 512)
                                out = bank[:, 2 * c + p0 // 512, 0:p1 - p0]
                                a = cut(qT, rows, slice(t * P, (t + 1) * P))
                                b = cut(kT, rows, slice(p0, p1))
                                diagonal = p1 == n
                                nc.tensor.matmul(out, a[0], b[0], start=True, stop=False)
                                nc.tensor.matmul(out, a[1], b[0], start=False, stop=False)
                                mm = nc.tensor.matmul(out, a[0], b[1], start=False, stop=not diagonal)
                                if diagonal:
                                    mm = nc.tensor.matmul(bank[:, 2 * c + p0 // 512, n - P - p0:n - p0], ident_r[:],
                                                          mask_r[:], start=False, stop=True)
                            mm.then_inc(score_full, 1)
                    if s == POOL_STEP and projects:
                        pool_project(h, 0, range(8))
                    there, t, u, _ = lagged(h, s, 2)
                    if there:
                        pe.wait_ge(v_ready, u + 1)
                        wait(pe, out_free, u)
                        for k in range(t + 1):
                            if k == 0:
                                pe.wait_ge(tb_free, tb)
                            if k == 4:
                                pe.wait_ge(ta_free, ta)
                            hi, lo = (wT[k // 4][i][:, k % 4, :] for i in range(2))
                            wide = (bank[:, OUT, 0:2 * P], hi, v_tok[:, k, :, :].rearrange("p a b -> p (a b)"))
                            narrow = (bank[:, OUT, 0:P], lo, v_tok[:, k, 0, :])
                            for i, m in enumerate((wide, narrow) if k == 0 else (narrow, wide)):
                                mm = nc.tensor.matmul(*m, start=k == 0 and i == 0, stop=k == t and i == 1)
                        mm.then_inc(out_full, 1)
                    there, t, u, _ = lagged(h, s, 3)
                    if there:
                        pe.wait_ge(a_normed, u + 1)
                        wait(pe, tb_free, tb)
                        nc.tensor.transpose(bank[:, TB, 0:P], attn_norm[t % 2][:], ident[:]).then_inc(tb_full, 1)
                        tb = tb + 1
                    if s == 0 and not first and projects:
                        project(h, 0, range(8))
                    if between:
                        between(s)

            pe.wait_ge(ident_ready, 1)
            pe.wait_ge(ident_r_ready, 2)
            pe.wait_ge(vec_in, 16 * 7)
            nc.tensor.transpose(bank[:, OUT, 0:N_ROWS], vec_rows[:], ident[0:N_ROWS, 0:N_ROWS]).then_inc(vec_full, 1)
            x_transpose(0)
            head(0)
            with pe.Fori(1, HEADS) as h:
                head(h)

            def gates(d, g, i):
                pe.wait_ge(w_ready, tile_block(d, g))
                if isinstance(d, int):
                    if (g, i) == (0, 0):
                        pe.wait_ge(proj_free, BANK_USES * HEADS)
                    else:
                        pe.wait_ge(exp_ready, 2 * T * HEADS)
                else:
                    pe.wait_ge(gate_ready, 4 * d)
                    if (g, i) == (1, 1):
                        pe.wait_ge(gated, 4 * d - 3)
                w = wblock(g)
                passes(bank[:, gate_bank(d, g, i), :], [(cut(w, ALL, k), cut(featT, ALL, k, HALVES[i]))
                                                        for k in range(KD)]).then_inc(gate_full, 1)

            def up_projections(d, br):
                pe.wait_ge(w_ready, tile_block(d, 2))
                w = wblock(2)
                src = (attnT, mixT)[br]
                for i in range(2):
                    n = 2 * br + i
                    if not isinstance(d, int):
                        pe.wait_ge(gated, 4 * (d - 1) + n + 1)
                    elif br == 0:
                        pe.wait_ge(exp_ready, 2 * T * HEADS)
                        pe.wait_ge(ta_free, 12 * HEADS)
                        pe.wait_ge(tb_free, 2 * T * HEADS)
                    else:
                        pe.wait_ge(mix_split, 2 * GROUPS)
                    passes(bank[:, up_bank(d, n), :], [(cut(w, ALL, 4 * br + k), cut(src, ALL, k, HALVES[i]))
                                                       for k in range(4)]).then_inc(up_full, 1)

            def pool_map(g):
                w = wblock(3)
                order = GROUP_ORDER.index(g)
                if order == 0:
                    pe.wait_ge(w_ready, POOL_W)
                    pe.wait_ge(tb_free, 2 * T * HEADS)
                    pe.wait_ge(out_free, T * HEADS)
                pe.wait_ge(pooled_split, order + 1)
                for i in range(2):
                    wait(pe, mix_split, 2 * (order - 1) + i + 1)
                    passes(bank[:, TB + i, :], [(cut(w, ALL, g), cut(pooledT, ALL, HALVES[i]))]).then_inc(mix_full, 1)

            def between(s):
                if s < 2:
                    gates(0, 0, s)
            head(HEADS, between)
            pool_map(0)
            gates(0, 1, 0)
            pool_map(1)
            gates(0, 1, 1)
            pool_map(3)
            up_projections(0, 0)
            pool_map(2)
            up_projections(0, 1)
            with pe.Fori(1, KD) as d:
                for g in range(2):
                    gates(d, g, 0)
                    gates(d, g, 1)
                up_projections(d, 0)
                up_projections(d, 1)

            def out_projection(t):
                pe.wait_ge(m_split, t + 1)
                for i in range(2):
                    n = 2 * t + i
                    if t == 0:
                        pe.wait_ge(gate_ready, 4 * KD)
                    wait(pe, res_ready, n - 3)
                    pairs = []
                    for k in range(KD):
                        w = (k4(slots[4 * i + k // 2][0], 2), k4(slots[4 * i + k // 2][1], 2))
                        pairs.append((cut(featT, ALL, k, slice(t * P, (t + 1) * P)), cut(w, ALL, k % 2)))
                    pe.wait_ge(w_ready, WO + 4 * i + 3)
                    passes(bank[:, n % 4, :], pairs).then_inc(wo_full, 1)

            def h2_transpose(t):
                pe.wait_ge(h2_ready, t + 1)
                if t < 2:
                    pe.wait_ge(gated, 4 * KD)
                for b in range(2):
                    wait(pe, h2T_split, 2 * (t - 2) + b + 1)
                    for k in range(4):
                        kk = 4 * b + k
                        mm = nc.tensor.transpose(bank[:, 4 + 2 * (t % 2) + b, k * P:(k + 1) * P],
                                                 h2_row[t % 2][:, kk * P:(kk + 1) * P], ident[:])
                    mm.then_inc(h2T_full, 1)

            for t in range(T):
                out_projection(t)
                if t:
                    h2_transpose(t - 1)

            def mlp_up(c):
                first = isinstance(c, int)
                for j in range(CH):
                    pe.wait_ge(w_ready, MLP0 + 8 * c + mlp_pos["in", j])
                    w = tuple(k4(part, 8) for part in mlp_slot("in", j))
                    for i in range(2):
                        n = 2 * j + i
                        if first and n == 0:
                            pe.wait_ge(res_ready, 2 * T)
                            pe.wait_ge(h2T_split, T)
                        if first and n == 1:
                            h2_transpose(T - 1)
                            pe.wait_ge(h2T_split, 2 * T)
                        wait(pe, relu_ready, 8 * c + n - 3)
                        passes(bank[:, n % 4, :], [(cut(w, ALL, k), cut(featT, ALL, k, HALVES[i]))
                                                   for k in range(KD)]).then_inc(u_done, 1)

            def mlp_down(c):
                pe.wait_ge(w_ready, MLP0 + 8 * c + 7)
                for t in range(T):
                    for i, half in enumerate(HALVES):
                        n = 2 * t + i
                        if n == 0:
                            pe.wait_ge(u_split, 8 * c + 4)
                        elif n > 3:
                            pe.wait_ge(y_added, 2 * T * c + n - 3)
                        pairs = [(cut(uT, ALL, j, slice(t * P, (t + 1) * P)),
                                  (slots[j][0][:, half], slots[j][1][:, half])) for j in range(CH)]
                        if t in (0, T // 2) and i == 0:
                            passes(bank[:, 4 + n % 4, :], pairs[:-1], stop=False)
                            pe.wait_ge(u_split, 8 * c + (7 if t == 0 else 8))
                            mm = passes(bank[:, 4 + n % 4, :], pairs[-1:], start=False)
                        else:
                            mm = passes(bank[:, 4 + n % 4, :], pairs)
                        mm.then_inc(down_full, 1)

            mlp_up(0)
            with pe.Fori(1, CHUNKS) as c:
                mlp_down(c - 1)
                mlp_up(c)
            mlp_down(CHUNKS - 1)


_INS = ["x", "norm1_g", "w_in", "b_gate", "q_norm_g", "k_norm_g", "lam_params", "subln_g", "pool_w", "pool_scale",
        "w_up_attn", "w_up_pool", "w_o", "norm2_g", "w_mlp_in", "w_mlp_out"]


def kernel(**inputs):
    import numpy as np
    import concourse.bacc as bacc
    from concourse.bass_utils import run_bass_kernel_spmd

    nc = bacc.Bacc("TRN2", target_bir_lowering=False, num_devices=1, dynamic_dma_scratch_size=1024)
    arrays, args = {}, []
    for name in _INS:
        a = np.ascontiguousarray(inputs[name])
        arrays[f"in_{name}"] = a
        args.append(nc.dram_tensor(f"in_{name}", a.shape, mybir.dt.from_np(a.dtype), kind="ExternalInput").ap())
    args.append(nc.dram_tensor("out_y", inputs["x"].shape, F32, kind="ExternalOutput").ap())
    trunk_layer(nc, *args)
    r = run_bass_kernel_spmd(nc, [arrays], core_ids=[0])
    return r.results[0]["out_y"]
```

```python
from contextlib import ExitStack

import concourse.bass as bass
from concourse import mybir

F32 = mybir.dt.float32
F32R = mybir.dt.float32r
ALU = mybir.AluOpType
ACT = mybir.ActivationFunctionType
AX = mybir.AxisListType

P = 128
KB = 1024


def trunk_layer(nc, x, norm1_g, w_in, b_gate, q_norm_g, k_norm_g, lam_params, subln_g,
                pool_w, pool_scale, w_up_attn, w_up_pool, w_o, norm2_g, w_mlp_in, w_mlp_out, y):
    _, SEQ, D = x.shape
    HEAD = q_norm_g.shape[1]
    VDIM = subln_g.shape[1]
    HEADS = w_up_attn.shape[1] // VDIM
    GROUPS = pool_w.shape[1]
    FF = w_mlp_in.shape[2]
    assert SEQ == D == 1024 and 2 * HEAD == VDIM == P and GROUPS == HEADS == 4
    EPS = 1e-6
    LAMBDA_INIT = 0.8 - 0.6
    NEG_BIG = -1e30
    T = SEQ // P
    KD = D // P
    HT = SEQ // 2
    CH = 4
    CHUNKS = FF // (CH * P)
    QK_COLS = HEADS * 2 * HEAD
    K0, V0 = QK_COLS, 2 * QK_COLS
    X0 = V0 + HEADS * VDIM
    G0 = X0 + GROUPS * P
    HALVES = (slice(0, HT), slice(HT, SEQ))

    x_rows = x.rearrange("b (t p) d -> (b t) p d", p=P)
    y_rows = y.rearrange("b (t p) d -> (b t) p d", p=P)
    w_in_v = w_in.rearrange("l (k p) c -> (l p) k c", p=P)
    up_a_v = w_up_attn.rearrange("l (k p) c -> (l p) k c", p=P)
    up_p_v = w_up_pool.rearrange("l (k p) c -> (l p) k c", p=P)
    w_o_v = w_o.rearrange("l (k p) c -> (l p) k c", p=P)
    mlp_in_v = w_mlp_in.rearrange("l (k p) c -> (l p) k c", p=P)
    mlp_out_v = w_mlp_out.rearrange("l (f p) c -> (l p) f c", p=P)
    pool_w_v = pool_w.rearrange("l g c d -> (l c) g d")

    with ExitStack() as ctx:
        BASE = 1152
        arena_used = []

        def at(name, kb, shape, dt=F32):
            off = BASE + int(kb * KB)
            size = 4
            for n in shape[1:]:
                size *= n
            arena_used.append(off + size)
            return nc.alloc_sbuf_tensor_at(name, shape, dt, offset=off)

        def both(name, kb, shape, apart):
            return (at(name + "_hi", kb, shape, F32R), at(name + "_lo", kb + apart, shape, F32R))

        featT = both("featT", 0, [P, KD, SEQ], 32)
        attnT = both("attnT", 64, [P, HEADS, SEQ], 16)
        h_row = [at(f"h_row{i}", 68 + 4 * i, [P, D]) for i in range(2)]
        g1_row = at("g1_row", 76, [P, D])
        square1 = at("square1", 84, [P, D])
        qT = both("qT", 96, [P, SEQ], 4)
        kT = both("kT", 104, [P, SEQ], 4)
        v_tok = at("v_tok", 112, [P, T, 2, P], F32R)
        wT = [both(f"wT{c}", 120 + 4 * c, [P, 4, P], 2) for c in range(2)]
        xpT = at("xpT", 128, [P, GROUPS, SEQ])
        x_tile = [at(f"x_tile{i}", 128 + 4 * i, [P, D]) for i in range(4)]
        prob = [at(f"prob{c}", 144 + 4 * c, [P, SEQ]) for c in range(2)]
        w_tok = at("w_tok", 152, [P, SEQ])
        qkv = [at(f"qkv{i}", kb, [P, 3 * P]) for i, kb in enumerate((156, 157.5, 221))]
        qk_norm = [at(f"qk_norm{i}", 208 + i, [P, 2 * P]) for i in range(2)]
        qk_square = at("qk_square", 210, [P, 4, HEAD])
        o_part = at("o_part", 212, [P, P])
        o_sum = [at(f"o_sum{i}", 212.5 + 0.5 * i, [P, P]) for i in range(2)]
        o_square = at("o_square", 213.5, [P, P])
        attn_norm = [at(f"attn_norm{i}", 214 + 0.5 * i, [P, P]) for i in range(2)]
        mixT = both("mixT", 96, [P, GROUPS, SEQ], 16)
        window = [at(f"window{i}", 144 + 4 * i, [P, SEQ]) for i in range(3)]
        POOL_GROUPS = (3, 2)
        wide_window = {g: [at(f"wide_window{g}_{i}", 96 + 4 * g + 16 * ((i + g) % 2 == 0), [P, SEQ]) for i in range(2)]
                       for g in POOL_GROUPS}
        wide_steps = {3: 0, 2: 6}
        mergedT = at("mergedT", 128, [P, KD, SEQ])
        gate = at("gate", 208, [P, 2, SEQ])
        res = at("res", 64, [P, T, D])
        h2_row = [at(f"h2_row{i}", 144 + 4 * i, [P, D]) for i in range(2)]
        g2_row = at("g2_row", 152, [P, D])
        square2 = at("square2", 156, [P, D])
        uT = (at("uT_hi", 144, [P, CH, SEQ], F32R), at("uT_lo", 96, [P, CH, SEQ], F32R))
        relu = [at(f"relu{i}", 208 + 2 * i, [P, HT]) for i in range(2)]
        u_full = [at(f"u_full{i}", 212 + 2 * i, [P, HT]) for i in range(2)]
        BLOCK = 1024
        raw = [at(f"raw{i}", 192 + 4 * i, [P, BLOCK]) for i in range(4)]
        slot_hi = at("slot_hi", 160, [P, 4, BLOCK], F32R)
        slot_lo = at("slot_lo", 176, [P, 4, BLOCK], F32R)
        more_hi = at("more_hi", 96, [P, 4, BLOCK], F32R)
        more_lo = at("more_lo", 112, [P, 4, BLOCK], F32R)
        in_hi = at("in_hi", 128, [P, 2, BLOCK], F32R)
        in_lo = at("in_lo", 136, [P, 2, BLOCK], F32R)
        slots = [(slot_hi[:, i], slot_lo[:, i]) for i in range(4)]
        slots += [(more_hi[:, i], more_lo[:, i]) for i in range(4)]
        slots += [(in_hi[:, i], in_lo[:, i]) for i in range(2)]
        ident = at("ident", 216, [P, P])
        mask = at("mask", 217, [P, P])
        N_ROWS = 2 * D // P + GROUPS + 3
        vec_rows = at("vec_rows", 218, [N_ROWS, P])
        col = at("col", 218.5, [P, N_ROWS])
        lam_in = at("lam_in", 218.75, [P, 4, HEAD])
        lam_prod = at("lam_prod", 219.75, [P, 2, HEAD])
        small = at("small", 220.25, [P, 128])
        BG, PS, SG, QG, KG = 0, 2 * D // P, 2 * D // P + GROUPS, 2 * D // P + GROUPS + 1, 2 * D // P + GROUPS + 2

        def sm(a, n=1):
            return small[:, a:a + n]

        neg_half, lam_sum, lam_exp, neg_lam, k_scale, sub_scale = sm(0, 4), sm(4, 2), sm(6, 2), sm(8), sm(9), sm(10)
        x_ss, x_ms, x_rstd = sm(12, 8), sm(20, 8), sm(28, 8)
        qk_ss = [sm(36 + 4 * i, 4) for i in range(2)]
        qk_ms = sm(44, 4)
        qk_rstd = [sm(48 + 4 * i, 4) for i in range(2)]
        neg_max = [sm(56 + 2 * i, 2) for i in range(2)]
        exp_sum = [sm(60 + 2 * i, 2) for i in range(2)]
        recip = [sm(92 + 2 * i, 2) for i in range(4)]
        coef = sm(68)
        a_ss, a_ms, a_rstd = sm(69), sm(70), sm(71)
        a_scale = [sm(72 + i) for i in range(2)]
        lam_diff = sm(75)
        count_inv = sm(76, 16)
        assert max(arena_used) <= nc.sbuf_usable_end

        bank = ctx.enter_context(nc.psum_tensor("bank", [P, 8, 512], F32))
        PROJ, TA, TB, OUT = 4, 5, 6, 7

        sems = {}

        def sem(name):
            sems[name] = ctx.enter_context(nc.semaphore(name))
            return sems[name]

        passed = sem("passed")
        raw_in = [sem(f"raw_in{i}") for i in range(4)]
        x_in = [sem(f"x_in{i}") for i in range(4)]
        res_in = sem("res_in")
        vec_in, lam_sem, g1_in, g2_in, y_out = sem("vec_in"), sem("lam_sem"), sem("g1_in"), sem("g2_in"), sem("y_out")
        zeroed, const_ready, ident_ready, mask_ready = (sem(n) for n in (
            "zeroed", "const_ready", "ident_ready", "mask_ready"))
        vec_full, col_ready, lam_step, lam_exped = (sem(n) for n in ("vec_full", "col_ready", "lam_step", "lam_exped"))
        w_hi, w_ready = sem("w_hi"), sem("w_ready")
        x_squared, x_mean, x_inv, h_ready, xT_full, xT_hi, xT_split = (sem(n) for n in (
            "x_squared", "x_mean", "x_inv", "h_ready", "xT_full", "xT_hi", "xT_split"))
        (proj_full, proj_free, qk_squared, qk_summed, qk_mean, qk_inv, qk_normed, v_hi, v_ready,
         ta_full, ta_hi, ta_free, tb_full, tb_hi, tb_free, score_full, max_ready, exp_ready, recip_ready,
         coef_ready, w_tok_ready, out_full, out_part, out_free, a_squared, a_mean, a_inv, a_scaled,
         a_normed) = (sem(n) for n in (
             "proj_full", "proj_free", "qk_squared", "qk_summed", "qk_mean", "qk_inv", "qk_normed", "v_hi",
             "v_ready", "ta_full", "ta_hi", "ta_free", "tb_full", "tb_hi", "tb_free", "score_full",
             "max_ready", "exp_ready", "recip_ready", "coef_ready", "w_tok_ready", "out_full", "out_part",
             "out_free", "a_squared", "a_mean", "a_inv", "a_scaled", "a_normed"))
        masked = sem("masked")
        wide_step = sem("wide_step")
        (pool_step, pooled_ready, pooled_hi, pooled_split, mix_full, mix_hi, mix_split, gate_full, gate_ready,
         up_full, gated, merged_ready) = (sem(n) for n in (
             "pool_step", "pooled_ready", "pooled_hi", "pooled_split", "mix_full", "mix_hi", "mix_split",
             "gate_full", "gate_ready", "up_full", "gated", "merged_ready"))
        m_first = sem("m_first")
        (m_hi, m_split, wo_full, res_ready, r_squared, r_mean, r_inv, h2_ready, h2T_full, h2T_hi,
         h2T_split) = (sem(n) for n in (
             "m_hi", "m_split", "wo_full", "res_ready", "r_squared", "r_mean", "r_inv", "h2_ready", "h2T_full",
             "h2T_hi", "h2T_split"))
        u_done, relu_ready, u_hi_ready, u_sq_ready, u_split, down_full, y_added = (sem(n) for n in (
            "u_done", "relu_ready", "u_hi_ready", "u_sq_ready", "u_split", "down_full", "y_added"))

        def wait(eng, s, value):
            if not isinstance(value, int) or value > 0:
                eng.wait_ge(s, value)

        def apart(eng):
            eng.sem_inc(passed, 1)

        def steps(h):
            return 4 if isinstance(h, int) and h == HEADS else T

        def lagged(h, s, lag):
            there = s < steps(h) and not (isinstance(h, int) and (s < lag if h == 0 else h == HEADS and s >= lag))
            return there, (s - lag) % T, T * h + s - lag, (h if s >= lag else h - 1)

        def at_head(h, per_head, missing):
            return 0 if isinstance(h, int) and h == 0 else per_head * h - missing

        def x_bank(t, b):
            return 2 * b + (t != 1)

        POOL_STEP = 5
        BANK_USES = T + 2

        def use_of(h, t):
            return BANK_USES * h + t + 1 + (t > POOL_STEP)

        X_TILES = ((1, 2), (3,), (4,), (5,), (6,), (7,))

        PIECES = (1, 1, 2)
        POOL_W, WO, MLP0 = 4 * HEADS + 4, 3 * KD + 18, 3 * KD + 26
        MLP_ORDER = [("in", 0), ("in", 1), ("out", 0), ("in", 2), ("out", 1), ("in", 3), ("out", 2), ("out", 3)]
        mlp_pos = {key: i for i, key in enumerate(MLP_ORDER)}

        def tile_block(d, i):
            return 4 * HEADS + 1 + i if isinstance(d, int) and d == 0 else 3 * d + 18 + i

        GROUP_ORDER = (0, 1, 3, 2)

        def window_of(g):
            return wide_window[g][g % 2] if g in POOL_GROUPS else window[g]

        def gate_bank(d, g, i):
            return (4, 0, 1, 2)[2 * g + i] if isinstance(d, int) else 2 * g + i

        def mix_bank(n, i):
            return (6 if n % 2 == 0 else 4) + i

        def up_bank(d, n):
            return (3, 0, 6, 7)[n] if isinstance(d, int) else 4 + n

        def k4(ap, n):
            return ap.rearrange("p (k c) -> p k c", k=n)

        def up_order(c):
            first = isinstance(c, int) and c == 0
            return [(0, 0), (1, 0), (0, 1), (1, 1)] * first + [(j, i) for j in range(2 * first, CH) for i in range(2)]

        def next_weights(c, q):
            first = isinstance(c, int) and c == 0
            return {2 if first else 1: (("in", 2), ("out", 1)), 3: (("in", 3), ("out", 2)), 5: (("out", 3),)}.get(q, ())

        def mlp_slot(kind, j):
            return slots[8 + j % 2] if kind == "in" else slots[j]

        block = ctx.enter_context(nc.Block())

        @block.sync
        def _(sp):
            def load(r, src, number, parts=8, behind=4, pieces=1):
                wait(sp, w_ready, number - behind)
                if not isinstance(number, int):
                    apart(sp)
                dst, n = k4(raw[r][:], parts), parts // pieces
                for i in range(pieces):
                    sp.dma_start(dst[:, n * i:n * i + n], src[:, n * i:n * i + n]).then_inc(raw_in[r], 16)

            def load_head(h):
                for i, c0 in enumerate((0, K0, V0)):
                    load(i, w_in_v[:, :, bass.ds(c0 + h * P, P)], 4 * h + 1 + i, pieces=PIECES[i])
                load(3, w_in_v[:, :, bass.ds(X0 + (GROUPS - 1 - h) * P, P)], 4 * h + 4)

            def load_tile(d, behind):
                load(0, w_in_v[:, :, bass.ds(G0 + d * P, P)], tile_block(d, 0), behind=behind)
                load(1, w_in_v[:, :, bass.ds(G0 + D + d * P, P)], tile_block(d, 1), behind=behind)
                sp.wait_ge(w_ready, tile_block(d, 2) - behind)
                apart(sp)
                up = k4(raw[2][:], 8)
                sp.dma_start(up[:, 0:4], up_a_v[:, :, bass.ds(d * P, P)]).then_inc(raw_in[2], 16)
                sp.dma_start(up[:, 4:8], up_p_v[:, :, bass.ds(d * P, P)]).then_inc(raw_in[2], 16)

            def load_chunk(c):
                for i, (kind, j) in enumerate(MLP_ORDER):
                    if kind == "in":
                        load(i % 4, mlp_in_v[:, :, bass.ds((c * CH + j) * P, P)], MLP0 + 8 * c + i)
                    else:
                        load(i % 4, mlp_out_v[:, bass.ds(c * CH + j, 1), :], MLP0 + 8 * c + i, parts=1)

            sp.dma_start(x_tile[0][:], x_rows[0]).then_inc(x_in[0], 16)
            for i, c0 in enumerate((0, K0, V0)):
                load(i, w_in_v[:, :, c0:c0 + P], 1 + i, pieces=PIECES[i])
                if i == 0:
                    sp.dma_start(g1_row[:], norm1_g.to_broadcast([P, D])).then_inc(g1_in, 16)
            sp.dma_start(x_tile[1][:], x_rows[1]).then_inc(x_in[1], 16)
            sp.dma_start(x_tile[2][:], x_rows[2]).then_inc(x_in[2], 16)
            rows_of = lambda v: v.rearrange("l (j p) -> (l j) p", p=P)
            sp.dma_start(vec_rows[BG:PS, :], rows_of(b_gate)).then_inc(vec_in, 16)
            sp.dma_start(vec_rows[PS:SG, :], rows_of(pool_scale)).then_inc(vec_in, 16)
            sp.dma_start(vec_rows[SG:SG + 1, :], subln_g).then_inc(vec_in, 16)
            for r, g in ((QG, q_norm_g), (KG, k_norm_g)):
                for c in range(2):
                    sp.dma_start(vec_rows[r:r + 1, c * HEAD:(c + 1) * HEAD], g).then_inc(vec_in, 16)
            sp.dma_start(lam_in[:].rearrange("p a b -> p (a b)"),
                         lam_params.rearrange("l a b -> l (a b)").to_broadcast([P, 4 * HEAD])).then_inc(lam_sem, 16)
            sp.dma_start(x_tile[3][:], x_rows[3]).then_inc(x_in[3], 16)
            for t in range(4, T):
                sp.wait_ge(h_ready, t - 3)
                sp.dma_start(x_tile[t % 4][:], x_rows[t]).then_inc(x_in[t % 4], 16)
            load(3, w_in_v[:, :, X0 + (GROUPS - 1) * P:X0 + GROUPS * P], 4)
            with sp.Fori(1, HEADS) as h:
                load_head(h)
            load_tile(0, 4)
            sp.wait_ge(w_ready, POOL_W - 4)
            sp.dma_start(k4(raw[3][:, 0:GROUPS * P], GROUPS), pool_w_v).then_inc(raw_in[3], 16)
            with sp.Fori(1, KD) as d:
                load_tile(d, 3)
            for b in range(8):
                k = 2 * (b % 4)
                c0 = (b // 4) * 512
                load(b % 4, w_o_v[:, k:k + 2, c0:c0 + 512], WO + b, parts=2, behind=3 if b < 4 else 4,
                     pieces=2 if b == 2 else 1)
            sp.wait_ge(up_full, 4 * KD)
            for t in range(T):
                sp.dma_start(res[:, t, :], x_rows[t]).then_inc(res_in, 16)
            sp.wait_ge(m_split, T - 1)
            sp.wait_ge(m_first, 2)
            sp.dma_start(g2_row[:], norm2_g.to_broadcast([P, D])).then_inc(g2_in, 16)
            load_chunk(0)
            with sp.Fori(1, CHUNKS) as c:
                load_chunk(c)
            for t in range(T):
                sp.wait_ge(y_added, 2 * T * (CHUNKS - 1) + 2 * t + 2)
                sp.dma_start(y_rows[t], res[:, t, :]).then_inc(y_out, 16)
            sp.wait_ge(y_out, 16 * T)

        @block.gpsimd
        def _(pool):
            pool.memset(ident[:], 0.0).then_inc(zeroed, 1)
            pool.memset(mask[:], 0.0).then_inc(zeroed, 1)
            pool.memset(neg_half, -0.5).then_inc(const_ready, 1)
            pool.wait_ge(zeroed, 2)
            pool.affine_select(out=ident[:], in_=ident[:], compare_op=ALU.not_equal, fill=1.0, base=0,
                               pattern=[[-1, P]], channel_multiplier=1).then_inc(ident_ready, 1)
            pool.affine_select(out=mask[:], in_=mask[:], compare_op=ALU.is_ge, fill=NEG_BIG, base=0,
                               pattern=[[-1, P]], channel_multiplier=1).then_inc(mask_ready, 1)
            pool.wait_ge(const_ready, 1)

            def inverse_root(ss, n_mean, ms, out, n, src, src_n, mean_sem, mean_n, inv_sem):
                pool.wait_ge(src, src_n)
                apart(pool)
                pool.tensor_scalar(ms, ss, 1.0 / n_mean, EPS, ALU.mult, ALU.add).then_inc(mean_sem, 1)
                pool.wait_ge(mean_sem, mean_n)
                pool.tensor_tensor(out, ms, neg_half[:, 0:n], ALU.pow).then_inc(inv_sem, 1)

            def x_inverse(t, squared, mean, inv):
                inverse_root(x_ss[:, t:t + 1], D, x_ms[:, t:t + 1], x_rstd[:, t:t + 1], 1, squared, t + 1, mean, t + 1, inv)

            def output_scale(t, u):
                wait(pool, a_normed, u - 1)
                inverse_root(a_ss, VDIM, a_ms, a_rstd, 1, a_squared, u + 1, a_mean, u + 1, a_inv)
                pool.wait_ge(a_inv, u + 1)
                pool.tensor_tensor(a_scale[t % 2], a_rstd, recip[t % 4][:, 0:1], ALU.mult).then_inc(a_scaled, 1)

            def split_v(h, s):
                there, t, u, of = lagged(h, s, 2)
                if not there:
                    return
                if t == 0:
                    wait(pool, out_full, T * of)
                pool.wait_ge(proj_free, use_of(of, t))
                apart(pool)
                v = qkv[t % 3][:, 2 * P:3 * P]
                pool.tensor_copy(v_tok[:, t, 0, :], v).then_inc(v_hi, 1)
                pool.wait_ge(v_hi, u + 1)
                pool.tensor_tensor(v_tok[:, t, 1, :], v, v_tok[:, t, 0, :], ALU.subtract).then_inc(v_ready, 1)

            def wide_sums(g, rounds):
                for i in rounds:
                    sh = 1 << i
                    now, into = (xpT[:, g, :] if i == 0 else wide_window[g][(i - 1) % 2]), wide_window[g][i % 2]
                    if i == 0:
                        pool.wait_ge(score_full, 2 * T * HEADS)
                        pool.wait_ge(proj_free, BANK_USES * HEADS)
                    else:
                        pool.wait_ge(wide_step, wide_steps[g] + 2 * i)
                    pool.tensor_copy(into[:, 0:sh], now[:, 0:sh]).then_inc(wide_step, 1)
                    pool.tensor_tensor(into[:, sh:], now[:, sh:], now[:, 0:SEQ - sh], ALU.add).then_inc(wide_step, 1)

            def head(h):
                for s in range(steps(h)):
                    if isinstance(h, int) and h == 0 and s < len(X_TILES):
                        for t in X_TILES[s]:
                            if t + 2 < T:
                                x_inverse(t + 2, x_squared, x_mean, x_inv)
                    there, t, u, _ = lagged(h, s, 4)
                    if there:
                        output_scale(t, u)
                    if s < 2:
                        split_v(h, s)
                    there, t, u, _ = lagged(h, s, 0)
                    if there:
                        wait(pool, qk_normed, u - 1)
                        inverse_root(qk_ss[t % 2], HEAD, qk_ms, qk_rstd[t % 2], 4,
                                     qk_summed, u + 1, qk_mean, u + 1, qk_inv)
                    if s >= 2:
                        split_v(h, s)
                    if s == 1 and steps(h) < T:
                        wide_sums(3, range(1))

            for t in range(3):
                x_inverse(t, x_squared, x_mean, x_inv)
            head(0)
            with pool.Fori(1, HEADS) as h:
                head(h)
            head(HEADS)
            pool.wait_ge(out_full, T * HEADS)
            wide_sums(3, range(1, 3))
            wide_sums(2, range(3))

            for i, tiles in enumerate((slice(0, KD - 1), slice(KD - 1, KD))):
                pool.wait_ge(m_hi, i + 1)
                pool.tensor_tensor(featT[1][:, tiles, 0:P], mergedT[:, tiles, 0:P], featT[0][:, tiles, 0:P],
                                   ALU.subtract).then_inc(m_first, 1)
            for t in range(T):
                x_inverse(t, r_squared, r_mean, r_inv)

        @block.scalar
        def _(act):
            def split_hi(number, r, loads, slot, used=None, used_n=0, width=BLOCK):
                act.wait_ge(raw_in[r], 16 * loads)
                if used is not None:
                    wait(act, used, used_n)
                nc.scalar.activation(slot[0][:, 0:width], raw[r][:, 0:width], ACT.Copy).then_inc(w_hi, 1)

            def x_square(t):
                act.wait_ge(x_in[t % 4], 16 * (t // 4 + 1))
                wait(act, x_squared, t)
                nc.scalar.activation(square1[:], x_tile[t % 4][:], ACT.Square,
                                     accum_out=x_ss[:, t:t + 1]).then_inc(x_squared, 1)

            def x_hi(t):
                for b in range(2):
                    act.wait_ge(xT_full, 2 * t + b + 1)
                    nc.scalar.activation(featT[0][:, 4 * b:4 * b + 4, t * P:(t + 1) * P],
                                         k4(bank[:, x_bank(t, b), :], 4), ACT.Copy).then_inc(xT_hi, 1)

            def take_projection(h, s):
                there, t, u, _ = lagged(h, s, 0)
                if there:
                    act.wait_ge(proj_full, use_of(h, t))
                    wait(act, qk_normed, u - 1 if t < 2 else u - 2)
                    wait(act, v_ready, u - 1 if t < 2 else u - 2)
                    nc.scalar.activation(qkv[t % 3][:], bank[:, PROJ, 0:3 * P], ACT.Copy).then_inc(proj_free, 1)

            def square_qk(h, s):
                there, t, u, _ = lagged(h, s, 0)
                if there:
                    act.wait_ge(proj_free, use_of(h, t))
                    wait(act, qk_summed, u)
                    nc.scalar.activation(qk_square[:].rearrange("p a b -> p (a b)"), qkv[t % 3][:, 0:2 * P],
                                         ACT.Square).then_inc(qk_squared, 1)

            def head_weights(h, i):
                split_hi(4 * h + 5 + i, i, PIECES[i] * (h + 2), slots[i], proj_full, use_of(h, T - 1))

            def exponential(c, t, u):
                n = (t + 1) * P
                act.wait_ge(max_ready, 2 * u + c + 1)
                wait(act, w_tok_ready, u)
                nc.scalar.activation(prob[c][:, 0:n], bank[:, 2 * c:2 * c + 2, :].rearrange("p a b -> p (a b)")[:, 0:n],
                                     ACT.Exp, bias=neg_max[t % 2][:, c:c + 1],
                                     accum_out=exp_sum[t % 2][:, c:c + 1]).then_inc(exp_ready, 1)

            def take_pool(use, g, i):
                act.wait_ge(proj_full, use)
                apart(act)
                nc.scalar.activation(xpT[:, bass.ds(g, 1), i * HT:(i + 1) * HT], bank[:, PROJ:PROJ + 1, :],
                                     ACT.Copy).then_inc(proj_free, 1)

            def head(h, between=None):
                first = isinstance(h, int) and h == 0
                ta, tb = at_head(h, 12, 7), at_head(h, 2 * T, 4)
                for s in range(steps(h)):
                    if first and s < len(X_TILES):
                        for t in X_TILES[s]:
                            if t + 2 < T:
                                x_square(t + 2)
                            x_hi(t)
                    there, t, u, _ = lagged(h, s, 4)
                    if there:
                        act.wait_ge(out_free, u + 1)
                        wait(act, a_mean, u)
                        wait(act, a_squared, u)
                        nc.scalar.activation(o_square[:], o_sum[t % 2][:], ACT.Square, scale=recip[t % 4][:, 0:1],
                                             accum_out=a_ss).then_inc(a_squared, 1)
                    soft, ts, us, _ = lagged(h, s, 2)
                    there, t, u, _ = lagged(h, s, 3)
                    long_rows = soft and ts >= 3
                    if soft and not long_rows:
                        exponential(0, ts, us)
                    if there:
                        act.wait_ge(tb_full, tb + 1)
                        wait(act, out_full, u)
                        n = min(t + 1, 4)
                        nc.scalar.activation(wT[0][0][:, 0:n, :], k4(bank[:, TB, 0:n * P], n), ACT.Copy).then_inc(tb_hi, 1)
                        tb = tb + 1
                    if long_rows:
                        exponential(0, ts, us)
                    if there and t >= 4:
                        act.wait_ge(ta_full, ta + 1)
                        nc.scalar.activation(wT[1][0][:, 0:t - 3, :], k4(bank[:, TA, 0:(t - 3) * P], t - 3),
                                             ACT.Copy).then_inc(ta_hi, 1)
                        ta = ta + 1
                    if soft:
                        exponential(1, ts, us)
                    if s == 0 and not first:
                        take_pool(BANK_USES * h, GROUPS - h, 1)
                    else:
                        take_projection(h, s)
                        square_qk(h, s)
                    there, t, u, _ = lagged(h, s, 1)
                    if there:
                        act.wait_ge(tb_full, tb + 1)
                        if t == 0:
                            wait(act, score_full, 2 * T * h)
                        if first and t == 0:
                            act.wait_ge(col_ready, 3)
                        sl = slice(t * P, (t + 1) * P)
                        nc.scalar.activation(qT[0][:, sl], bank[:, TB, 0:P], ACT.Copy).then_inc(tb_hi, 1)
                        nc.scalar.activation(kT[0][:, sl], bank[:, TB, P:2 * P], ACT.Copy,
                                             scale=k_scale).then_inc(tb_hi, 1)
                        tb = tb + 1
                    there, t, u, _ = lagged(h, s, 3)
                    if there:
                        act.wait_ge(out_full, u + 1)
                        wait(act, out_free, u)
                        nc.scalar.activation(o_part[:], bank[:, OUT, P:2 * P], ACT.Copy).then_inc(out_part, 1)
                    there, t, u, of = lagged(h, s, 4)
                    if there:
                        act.wait_ge(ta_full, ta + 1)
                        apart(act)
                        nc.scalar.activation(attnT[0][:, bass.ds(of, 1), t * P:(t + 1) * P], bank[:, TA:TA + 1, 0:P],
                                             ACT.Copy, scale=sub_scale).then_inc(ta_hi, 1)
                        ta = ta + 1
                    if s == 0 and not first:
                        take_projection(h, s)
                        square_qk(h, s)
                    if first and s == 0:
                        act.wait_ge(lam_step, 2)
                        nc.scalar.activation(lam_exp, lam_sum, ACT.Exp).then_inc(lam_exped, 1)
                    if s == POOL_STEP and s < steps(h):
                        if first:
                            act.wait_ge(h_ready, T)
                        take_pool(BANK_USES * h + POOL_STEP + 2, GROUPS - 1 - h, 0)
                    if s == 2 and steps(h) == T:
                        split_hi(4 * h + 4, 3, h + 1, slots[3], proj_full, BANK_USES * h)
                    if s == T - 1:
                        for i in range(3):
                            head_weights(h, i)
                    if between:
                        between(s)

            x_square(0)
            for i in range(3):
                split_hi(1 + i, i, PIECES[i], slots[i])
                if i == 1:
                    x_hi(0)
            x_square(1)
            x_square(2)
            head(0)
            with act.Fori(1, HEADS) as h:
                head(h)

            def gates(d, g, i):
                act.wait_ge(gate_full, 4 * d + 2 * g + i + 1)
                wait(act, merged_ready, 2 * d)
                apart(act)
                nc.scalar.activation(gate[:, g, HALVES[i]], bank[:, gate_bank(d, g, i), :], ACT.Sigmoid,
                                     bias=col[:, bass.ds(BG + KD * g + d, 1)]).then_inc(gate_ready, 1)

            def next_tile(d, i):
                used = (gate_full, 4 * d + 2 * i + 2) if i < 2 else (up_full, 4 * d + 4)
                split_hi(3 * d + 21 + i, i, PIECES[i] * (HEADS + 2 + d), slots[i], *used)

            def pooled_hi_part(g):
                n = GROUP_ORDER.index(g)
                act.wait_ge(pooled_ready, n + 1)
                nc.scalar.activation(mixT[0][:, g, :], window_of(g)[:], ACT.Copy).then_inc(pooled_hi, 1)

            def mix_hi_part(g):
                n = GROUP_ORDER.index(g)
                for i, half in enumerate(HALVES):
                    act.wait_ge(mix_full, 2 * n + i + 1)
                    nc.scalar.activation(mixT[0][:, g, half], bank[:, mix_bank(n, i), :], ACT.Copy,
                                         scale=col[:, PS + g:PS + g + 1]).then_inc(mix_hi, 1)

            def between(s):
                if s == 1:
                    split_hi(POOL_W, 3, HEADS + 1, slots[3], proj_full, BANK_USES * HEADS, width=GROUPS * P)
                    gates(0, 0, 0)
                if s == 2:
                    gates(0, 0, 1)
                    next_tile(0, 0)
                    pooled_hi_part(0)
            head(HEADS, between)
            pooled_hi_part(1)
            gates(0, 1, 0)
            mix_hi_part(0)
            mix_hi_part(1)
            gates(0, 1, 1)
            pooled_hi_part(3)
            next_tile(0, 1)
            mix_hi_part(3)
            pooled_hi_part(2)
            mix_hi_part(2)
            with act.Fori(1, KD) as d:
                for g in range(2):
                    gates(d, g, 0)
                    if g == 0:
                        next_tile(d - 1, 2)
                    gates(d, g, 1)
                    next_tile(d, g)

            def merged_hi(t, tiles=slice(0, KD)):
                nc.scalar.activation(featT[0][:, tiles, t * P:(t + 1) * P], mergedT[:, tiles, t * P:(t + 1) * P],
                                     ACT.Copy).then_inc(m_hi, 1)

            act.wait_ge(gate_full, 4 * KD)
            act.wait_ge(merged_ready, 2 * (KD - 1))
            merged_hi(0, slice(0, KD - 1))
            act.wait_ge(merged_ready, 2 * KD - 1)
            merged_hi(0, slice(KD - 1, KD))
            next_tile(KD - 1, 2)
            split_hi(WO + 3, 3, HEADS + 2, slots[3], mix_full, 2 * GROUPS)
            act.wait_ge(merged_ready, 2 * KD)
            act.wait_ge(up_full, 4 * KD)
            raw_loads = [HEADS + KD + 1, HEADS + KD + 1, PIECES[2] * (HEADS + KD + 1), HEADS + 2]
            for b in range(4):
                split_hi(WO + 4 + b, b, raw_loads[b] + 1, slots[4 + b])
            for t in range(1, T):
                merged_hi(t)

            def chunk_hi(c, kind, j, used, used_n):
                i = mlp_pos[kind, j]
                split_hi(MLP0 + 8 * c + i, i % 4, raw_loads[i % 4] + 2 * c + 2 + i // 4, mlp_slot(kind, j), used, used_n)

            def h2_hi(t):
                for b in range(2):
                    act.wait_ge(h2T_full, 2 * t + b + 1)
                    nc.scalar.activation(featT[0][:, 4 * b:4 * b + 4, t * P:(t + 1) * P],
                                         k4(bank[:, 4 + 2 * (t % 2) + b, :], 4), ACT.Copy).then_inc(h2T_hi, 1)

            for t in range(T):
                act.wait_ge(res_ready, 2 * t + 2)
                wait(act, r_squared, t)
                nc.scalar.activation(square2[:], res[:, t, :], ACT.Square,
                                     accum_out=x_ss[:, t:t + 1]).then_inc(r_squared, 1)
                if t == 2:
                    chunk_hi(0, "in", 0, m_split, T - 1)
                    chunk_hi(0, "in", 1, m_split, T - 1)
                if t > 1:
                    h2_hi(t - 2)

            def up(c):
                first = isinstance(c, int) and c == 0
                if first:
                    chunk_hi(c, "out", 0, wo_full, 2 * T)
                else:
                    chunk_hi(c, "out", 0, down_full, 2 * T * c)
                for q, (j, i) in enumerate(up_order(c)):
                    n = 8 * c + q
                    act.wait_ge(u_done, n + 1)
                    wait(act, u_sq_ready, n - 1)
                    nc.scalar.activation(relu[q % 2][:], bank[:, q % 4, :], ACT.Relu).then_inc(relu_ready, 1)
                    act.wait_ge(relu_ready, n + 1)
                    if first and q == 0:
                        act.wait_ge(h2_ready, T)
                        act.wait_ge(h2T_full, 2 * T)
                    nc.scalar.activation(uT[0][:, j, HALVES[i]], relu[q % 2][:], ACT.Square).then_inc(u_hi_ready, 1)
                    for kind, block_j in next_weights(c, q):
                        if kind == "in":
                            chunk_hi(c, kind, block_j, u_done, 8 * c + q + 1)
                        else:
                            chunk_hi(c, kind, block_j, None, 0)

            h2_hi(T - 2)
            h2_hi(T - 1)
            up(0)
            with act.Fori(1, CHUNKS) as c:
                chunk_hi(c, "in", 0, u_done, 8 * c - 2)
                chunk_hi(c, "in", 1, u_done, 8 * c)
                up(c)

        @block.vector
        def _(dve):
            def split_lo(number, r, slot, width=BLOCK):
                dve.wait_ge(w_hi, number)
                nc.vector.tensor_tensor(slot[1][:, 0:width], raw[r][:, 0:width], slot[0][:, 0:width],
                                        ALU.subtract).then_inc(w_ready, 1)

            def x_norm(t):
                dve.wait_ge(x_inv, t + 1)
                if t == 0:
                    dve.wait_ge(g1_in, 16)
                wait(dve, xT_full, 2 * (t - 1))
                nc.vector.scalar_tensor_tensor(h_row[t % 2][:], x_tile[t % 4][:], x_rstd[:, t:t + 1], g1_row[:],
                                               ALU.mult, ALU.mult).then_inc(h_ready, 1)

            def x_lo(t):
                for b in range(2):
                    dve.wait_ge(xT_hi, 2 * t + b + 1)
                    dst = (slice(None), slice(4 * b, 4 * b + 4), slice(t * P, (t + 1) * P))
                    nc.vector.tensor_tensor(featT[1][dst], k4(bank[:, x_bank(t, b), :], 4), featT[0][dst],
                                            ALU.subtract).then_inc(xT_split, 1)

            def head_weights(h, i):
                split_lo(4 * h + 5 + i, i, slots[i])

            def vectors():
                dve.wait_ge(lam_sem, 16)
                pairs = lam_in[:].rearrange("p (a b) c -> p a b c", b=2)
                nc.vector.tensor_tensor(lam_prod[:], pairs[:, :, 0, :], pairs[:, :, 1, :], ALU.mult).then_inc(lam_step, 1)
                dve.wait_ge(lam_step, 1)
                nc.vector.tensor_reduce(lam_sum, lam_prod[:], AX.X, ALU.add).then_inc(lam_step, 1)
                dve.wait_ge(lam_exped, 1)
                nc.vector.tensor_tensor(lam_diff, lam_exp[:, 1:2], lam_exp[:, 0:1], ALU.subtract).then_inc(lam_step, 1)
                dve.wait_ge(lam_step, 3)
                nc.vector.tensor_scalar(neg_lam, lam_diff, -LAMBDA_INIT, None, ALU.add).then_inc(lam_step, 1)
                dve.wait_ge(lam_step, 4)
                dve.wait_ge(vec_full, 1)
                nc.vector.tensor_copy(col[:], bank[:, OUT, 0:N_ROWS]).then_inc(col_ready, 1)
                dve.wait_ge(col_ready, 1)
                nc.vector.scalar_tensor_tensor(k_scale, col[:, QG:QG + 1], float(HEAD) ** -0.5, col[:, KG:KG + 1],
                                               ALU.mult, ALU.mult).then_inc(col_ready, 1)
                nc.vector.tensor_scalar(sub_scale, col[:, SG:SG + 1], 1.0 - LAMBDA_INIT, None,
                                        ALU.mult).then_inc(col_ready, 1)
                dve.wait_ge(col_ready, 3)

            def normalise_qk(h, s):
                there, t, u, _ = lagged(h, s, 1)
                if there:
                    dve.wait_ge(qk_inv, u + 1)
                    nc.vector.tensor_tensor(qk_norm[t % 2][:].rearrange("p (g c) -> p g c", c=HEAD),
                                            qkv[t % 3][:, 0:2 * P].rearrange("p (g c) -> p g c", c=HEAD),
                                            qk_rstd[t % 2].unsqueeze(2).to_broadcast([P, 4, HEAD]),
                                            ALU.mult).then_inc(qk_normed, 1)

            def sum_squares(h, s):
                there, t, u, _ = lagged(h, s, 0)
                if there:
                    dve.wait_ge(qk_squared, u + 1)
                    nc.vector.tensor_reduce(qk_ss[t % 2], qk_square[:], AX.X, ALU.add).then_inc(qk_summed, 1)

            def head(h, between=None):
                first = isinstance(h, int) and h == 0
                ta, tb_parts = at_head(h, 12, 7), at_head(h, 3 * T, 5)
                for s in range(steps(h)):
                    if first and s < len(X_TILES):
                        for t in X_TILES[s]:
                            if t + 1 < T:
                                x_norm(t + 1)
                            x_lo(t)
                    there, t, u, _ = lagged(h, s, 2)
                    late_scores = there and t >= 3
                    if late_scores:
                        normalise_qk(h, s)
                    for c in range(2):
                        if there:
                            n = (t + 1) * P
                            dve.wait_ge(score_full, 2 * u + c + 1)
                            diagonal = bank[:, 2 * c + t // 4, t % 4 * P:(t % 4 + 1) * P]
                            nc.vector.tensor_tensor(diagonal, diagonal, mask[:], ALU.add).then_inc(masked, 1)
                            dve.wait_ge(masked, 2 * u + c + 1)
                            nc.vector.tensor_reduce(neg_max[t % 2][:, c:c + 1],
                                                    bank[:, 2 * c:2 * c + 2, :].rearrange("p a b -> p (a b)")[:, 0:n],
                                                    AX.X, ALU.max, negate=True).then_inc(max_ready, 1)
                    there, t, u, _ = lagged(h, s, 3)
                    if there:
                        n = min(t + 1, 4)
                        dve.wait_ge(tb_hi, tb_parts + 1)
                        nc.vector.tensor_tensor(wT[0][1][:, 0:n, :], k4(bank[:, TB, 0:n * P], n), wT[0][0][:, 0:n, :],
                                                ALU.subtract).then_inc(tb_free, 1)
                        tb_parts = tb_parts + 1
                    if not late_scores:
                        normalise_qk(h, s)
                    there, t, u, _ = lagged(h, s, 3)
                    if there and t >= 4:
                        dve.wait_ge(ta_hi, ta + 1)
                        nc.vector.tensor_tensor(wT[1][1][:, 0:t - 3, :], k4(bank[:, TA, 0:(t - 3) * P], t - 3),
                                                wT[1][0][:, 0:t - 3, :], ALU.subtract).then_inc(ta_free, 1)
                        ta = ta + 1
                    if s == 0 and not first:
                        head_weights(h - 1, 2)
                    there, t, u, _ = lagged(h, s, 4)
                    if there:
                        dve.wait_ge(a_scaled, u + 1)
                        nc.vector.tensor_scalar(attn_norm[t % 2][:], o_sum[t % 2][:], a_scale[t % 2], None,
                                                ALU.mult).then_inc(a_normed, 1)
                    there, t, u, _ = lagged(h, s, 2)
                    if there:
                        n = (t + 1) * P
                        dve.wait_ge(exp_ready, 2 * u + 2)
                        nc.vector.reciprocal(recip[t % 4], exp_sum[t % 2]).then_inc(recip_ready, 1)
                        dve.wait_ge(recip_ready, u + 1)
                        nc.vector.scalar_tensor_tensor(coef, exp_sum[t % 2][:, 0:1], neg_lam, recip[t % 4][:, 1:2],
                                                       ALU.mult, ALU.mult).then_inc(coef_ready, 1)
                        dve.wait_ge(coef_ready, u + 1)
                        nc.vector.scalar_tensor_tensor(w_tok[:, 0:n], prob[1][:, 0:n], coef, prob[0][:, 0:n],
                                                       ALU.mult, ALU.add).then_inc(w_tok_ready, 1)
                    if s > 0 or first:
                        sum_squares(h, s)
                    there, t, u, _ = lagged(h, s, 1)
                    if there:
                        sl = slice(t * P, (t + 1) * P)
                        dve.wait_ge(tb_hi, tb_parts + 2)
                        nc.vector.tensor_tensor(qT[1][:, sl], bank[:, TB, 0:P], qT[0][:, sl], ALU.subtract)
                        nc.vector.scalar_tensor_tensor(kT[1][:, sl], bank[:, TB, P:2 * P], k_scale, kT[0][:, sl],
                                                       ALU.mult, ALU.subtract).then_inc(tb_free, 1)
                        tb_parts = tb_parts + 2
                    there, t, u, _ = lagged(h, s, 3)
                    if there:
                        dve.wait_ge(out_part, u + 1)
                        nc.vector.tensor_tensor(o_sum[t % 2][:], bank[:, OUT, 0:P], o_part[:], ALU.add).then_inc(out_free, 1)
                    there, t, u, of = lagged(h, s, 4)
                    if there:
                        dve.wait_ge(ta_hi, ta + 1)
                        nc.vector.scalar_tensor_tensor(attnT[1][:, bass.ds(of, 1), t * P:(t + 1) * P],
                                                       bank[:, TA:TA + 1, 0:P], sub_scale,
                                                       attnT[0][:, bass.ds(of, 1), t * P:(t + 1) * P],
                                                       ALU.mult, ALU.subtract).then_inc(ta_free, 1)
                        ta = ta + 1
                    if s == 0 and not first:
                        sum_squares(h, s)
                    if first and s == 0:
                        vectors()
                    if s == 2 and steps(h) == T:
                        split_lo(4 * h + 4, 3, slots[3])
                    if s == T - 1:
                        head_weights(h, 0)
                        head_weights(h, 1)
                    if between:
                        between(s)

            dve.wait_ge(mask_ready, 1)
            for i in range(16):
                nc.vector.memset(count_inv[:, i:i + 1], 1.0 / (i + 1))
            x_norm(0)
            for i in range(3):
                split_lo(1 + i, i, slots[i])
                if i == 1:
                    x_lo(0)
            x_norm(1)
            head(0)
            with dve.Fori(1, HEADS) as h:
                head(h)

            step = [0]

            def pool_wait():
                dve.wait_ge(pool_step, step[0])

            def pool_inc(ins):
                step[0] += 1
                ins.then_inc(pool_step, 1)

            def sums(g):
                if g == 0:
                    dve.wait_ge(proj_free, BANK_USES * HEADS)
                    dve.wait_ge(w_tok_ready, T * HEADS)
                src = xpT[:, g, :]
                for i in range(g + 1):
                    sh = 1 << i
                    dst = window[g] if i == g else window[2]
                    pool_inc(nc.vector.tensor_copy(dst[:, 0:sh], src[:, 0:sh]))
                    pool_inc(nc.vector.tensor_tensor(dst[:, sh:], src[:, sh:], src[:, 0:SEQ - sh], ALU.add))
                    pool_wait()
                    src = dst

            def means(g):
                w = 2 << g
                src = window_of(g)
                if g in POOL_GROUPS:
                    dve.wait_ge(wide_step, wide_steps[g] + 6)
                if g == 3:
                    last = wide_window[g][0]
                    pool_inc(nc.vector.tensor_copy(src[:, 0:8], last[:, 0:8]))
                    pool_inc(nc.vector.tensor_tensor(src[:, 8:], last[:, 8:], last[:, 0:SEQ - 8], ALU.add))
                    pool_wait()
                if g not in POOL_GROUPS:
                    sums(g)
                pool_inc(nc.vector.tensor_tensor(src[:, 0:w - 1], src[:, 0:w - 1], count_inv[:, 0:w - 1], ALU.mult))
                pool_wait()
                nc.vector.tensor_tensor(src[:, 0:w - 1], src[:, 0:w - 1], xpT[:, g, 0:w - 1], ALU.subtract)
                nc.vector.scalar_tensor_tensor(src[:, w - 1:], src[:, w - 1:], 1.0 / w, xpT[:, g, w - 1:],
                                               ALU.mult, ALU.subtract).then_inc(pooled_ready, 1)

            def pooled_lo_part(g):
                n = GROUP_ORDER.index(g)
                if n == 0:
                    dve.wait_ge(out_full, T * HEADS)
                dve.wait_ge(pooled_ready, n + 1)
                dve.wait_ge(pooled_hi, n + 1)
                nc.vector.tensor_tensor(mixT[1][:, g, :], window_of(g)[:], mixT[0][:, g, :],
                                        ALU.subtract).then_inc(pooled_split, 1)

            def mix_lo_part(g):
                n = GROUP_ORDER.index(g)
                for i, half in enumerate(HALVES):
                    dve.wait_ge(mix_hi, 2 * n + i + 1)
                    nc.vector.scalar_tensor_tensor(mixT[1][:, g, half], bank[:, mix_bank(n, i), :],
                                                   col[:, PS + g:PS + g + 1], mixT[0][:, g, half],
                                                   ALU.mult, ALU.subtract).then_inc(mix_split, 1)

            def next_tile(d, i):
                split_lo(3 * d + 21 + i, i, slots[i])

            def merge(d, br, i, n):
                half = HALVES[i]
                dve.wait_ge(up_full, 4 * d + n + 1)
                dve.wait_ge(gate_ready, 4 * d + 2 * br + i + 1)
                nc.vector.tensor_tensor(gate[:, br, half], gate[:, br, half], bank[:, up_bank(d, 2 * br + i), :],
                                        ALU.mult).then_inc(gated, 1)
                if br == 1:
                    dve.wait_ge(gated, 4 * d + n + 1)
                    nc.vector.tensor_tensor(mergedT[:, bass.ds(d, 1), half], gate[:, 0:1, half],
                                            gate[:, 1:2, half], ALU.add).then_inc(merged_ready, 1)

            def between(s):
                if s == 1:
                    split_lo(POOL_W, 3, slots[3], width=GROUPS * P)
                    means(0)
                if s == 2:
                    means(1)
            head(HEADS, between)
            next_tile(0, 0)
            pooled_lo_part(0)
            pooled_lo_part(1)
            means(3)
            mix_lo_part(0)
            mix_lo_part(1)
            pooled_lo_part(3)
            means(2)
            pooled_lo_part(2)
            mix_lo_part(3)
            mix_lo_part(2)
            next_tile(0, 1)
            merge(0, 0, 0, 0)
            merge(0, 0, 1, 1)
            merge(0, 1, 0, 2)
            merge(0, 1, 1, 3)
            with dve.Fori(1, KD) as d:
                next_tile(d - 1, 2)
                next_tile(d, 0)
                next_tile(d, 1)
                for i in range(2):
                    merge(d, 0, i, 2 * i)
                    merge(d, 1, i, 2 * i + 1)
            next_tile(KD - 1, 2)

            def merged_lo(t):
                dst = (slice(None), slice(None), slice(t * P, (t + 1) * P))
                dve.wait_ge(m_hi, t + 2)
                nc.vector.tensor_tensor(featT[1][dst], mergedT[dst], featT[0][dst], ALU.subtract).then_inc(m_split, 1)

            split_lo(WO + 3, 3, slots[3])
            for b in range(4, 8):
                split_lo(WO + b, b % 4, slots[b])
            for t in range(1, T):
                merged_lo(t)

            def chunk_lo(c, kind, j):
                i = mlp_pos[kind, j]
                split_lo(MLP0 + 8 * c + i, i % 4, mlp_slot(kind, j))

            def h2_lo(t):
                for b in range(2):
                    dve.wait_ge(h2T_hi, 2 * t + b + 1)
                    dst = (slice(None), slice(4 * b, 4 * b + 4), slice(t * P, (t + 1) * P))
                    nc.vector.tensor_tensor(featT[1][dst], k4(bank[:, 4 + 2 * (t % 2) + b, :], 4), featT[0][dst],
                                            ALU.subtract).then_inc(h2T_split, 1)

            dve.wait_ge(res_in, 16 * T)
            for t in range(T):
                for i, half in enumerate(HALVES):
                    n = 2 * t + i
                    dve.wait_ge(wo_full, n + 1)
                    nc.vector.tensor_tensor(res[:, t, half], res[:, t, half], bank[:, n % 4, :],
                                            ALU.add).then_inc(res_ready, 1)
                if t == 2:
                    chunk_lo(0, "in", 0)
                    chunk_lo(0, "in", 1)
                if t > 1:
                    h2_lo(t - 2)
                if t == 0:
                    dve.wait_ge(g2_in, 16)
                dve.wait_ge(r_inv, t + 1)
                dve.wait_ge(res_ready, 2 * t + 2)
                wait(dve, h2T_full, 2 * (t - 1))
                nc.vector.scalar_tensor_tensor(h2_row[t % 2][:], res[:, t, :], x_rstd[:, t:t + 1], g2_row[:],
                                               ALU.mult, ALU.mult).then_inc(h2_ready, 1)

            def up(c):
                chunk_lo(c, "out", 0)
                for q, (j, i) in enumerate(up_order(c)):
                    n = 8 * c + q
                    dve.wait_ge(relu_ready, n + 1)
                    nc.vector.tensor_tensor(u_full[q % 2][:], relu[q % 2][:], relu[q % 2][:], ALU.mult).then_inc(u_sq_ready, 1)
                    dve.wait_ge(u_sq_ready, n + 1)
                    dve.wait_ge(u_hi_ready, n + 1)
                    nc.vector.tensor_tensor(uT[1][:, j, HALVES[i]], u_full[q % 2][:], uT[0][:, j, HALVES[i]],
                                            ALU.subtract).then_inc(u_split, 1)
                    for kind, block_j in next_weights(c, q):
                        chunk_lo(c, kind, block_j)

            def down(c, between=None):
                for t in range(T):
                    for i, half in enumerate(HALVES):
                        n = 2 * T * c + 2 * t + i
                        dve.wait_ge(down_full, n + 1)
                        nc.vector.tensor_tensor(res[:, t, half], res[:, t, half], bank[:, 4 + (2 * t + i) % 4, :],
                                                ALU.add).then_inc(y_added, 1)
                    if t == 0 and between:
                        between()

            h2_lo(T - 2)
            h2_lo(T - 1)
            dve.wait_ge(h2_ready, T)
            up(0)
            with dve.Fori(1, CHUNKS) as c:
                def next_in():
                    chunk_lo(c, "in", 0)
                    chunk_lo(c, "in", 1)
                down(c - 1, next_in)
                up(c)
            down(CHUNKS - 1)

        @block.tensor
        def _(pe):
            def passes(out, pairs, start=True, stop=True):
                steps = [(a, b) for (ah, al), (bh, bl) in pairs for a, b in ((ah, bh), (al, bh), (ah, bl))]
                for i, (a, b) in enumerate(steps):
                    mm = nc.tensor.matmul(out, a, b, start=start and i == 0, stop=stop and i == len(steps) - 1)
                return mm

            def cut(pair, *idx):
                return (pair[0][idx], pair[1][idx])

            ALL = slice(None)

            def wblock(i, n=8):
                return (k4(slots[i][0], n), k4(slots[i][1], n))

            def x_transpose(t):
                pe.wait_ge(h_ready, t + 1)
                for b in range(2):
                    if t > 1:
                        pe.wait_ge(xT_split, 2 * (t - 1 if t > 2 else 0) + b + 1)
                    for k in range(4):
                        kk = 4 * b + k
                        mm = nc.tensor.transpose(bank[:, x_bank(t, b), k * P:(k + 1) * P],
                                                 h_row[t % 2][:, kk * P:(kk + 1) * P], ident[:])
                    mm.then_inc(xT_full, 1)

            def project(h, t, ks):
                first = isinstance(h, int)
                if 0 in ks:
                    if t == 0:
                        pe.wait_ge(w_ready, 4 * h + 3)
                    if first:
                        pe.wait_ge(xT_split, 2 * t + 2)
                    wait(pe, proj_free, use_of(h, t) - 1)
                out = bank[:, PROJ, 0:3 * P].rearrange("p (m c) -> p m c", m=3)
                for k in ks:
                    a = cut(featT, ALL, k, slice(t * P, (t + 1) * P))
                    b = (slot_hi[:, 0:3, k * P:(k + 1) * P], slot_lo[:, 0:3, k * P:(k + 1) * P])
                    mm = passes(out, [(a, b)], start=k == 0, stop=k == KD - 1)
                if KD - 1 in ks:
                    mm.then_inc(proj_full, 1)

            def pool_project(h, i, ks):
                if 0 in ks:
                    pe.wait_ge(w_ready, 4 * h + 4)
                    pe.wait_ge(proj_free, BANK_USES * h + (POOL_STEP + 1 if i == 0 else BANK_USES - 1))
                w = wblock(3)
                for k in ks:
                    mm = passes(bank[:, PROJ, :], [(cut(w, ALL, k), cut(featT, ALL, k, HALVES[i]))],
                                start=k == 0, stop=k == KD - 1)
                if KD - 1 in ks:
                    mm.then_inc(proj_full, 1)

            def weights_transpose(t, c):
                n = min(t + 1, 4) if c == 0 else t - 3
                b = TB if c == 0 else TA
                for k in range(n):
                    mm = nc.tensor.transpose(bank[:, b, k * P:(k + 1) * P],
                                             w_tok[:, (4 * c + k) * P:(4 * c + k + 1) * P], ident[:])
                return mm

            def gates(d, g, i, ks=range(KD)):
                if 0 in ks:
                    pe.wait_ge(w_ready, tile_block(d, g))
                    if not isinstance(d, int):
                        pe.wait_ge(gate_ready, 4 * d)
                        if (g, i) == (0, 0):
                            pe.wait_ge(gated, 4 * d - 2)
                    elif (g, i) == (0, 0):
                        pe.wait_ge(proj_free, BANK_USES * HEADS)
                    else:
                        pe.wait_ge(exp_ready, 2 * T * HEADS - (i == 1 and g == 0))
                w = wblock(g)
                mm = passes(bank[:, gate_bank(d, g, i), :], [(cut(w, ALL, k), cut(featT, ALL, k, HALVES[i])) for k in ks],
                            start=0 in ks, stop=KD - 1 in ks)
                if KD - 1 in ks:
                    mm.then_inc(gate_full, 1)

            def scores(h, s, tb):
                there, t, u, _ = lagged(h, s, 2)
                if not there:
                    return
                n = (t + 1) * P
                pe.wait_ge(tb_free, tb)
                if isinstance(h, int) and h == 0 and t == 4:
                    pe.wait_ge(xT_split, 2 * T)
                for c in range(2):
                    wait(pe, exp_ready, 2 * (u - 1) + c + 1)
                for p0 in range(0, n, 512):
                    p1 = min(n, p0 + 512)
                    for i in range(3):
                        for c in range(2):
                            rows = slice(c * HEAD, (c + 1) * HEAD)
                            a = (qT[0], qT[1], qT[0])[i][rows, t * P:(t + 1) * P]
                            b = (kT[0], kT[0], kT[1])[i][rows, p0:p1]
                            mm = nc.tensor.matmul(bank[:, 2 * c + p0 // 512, 0:p1 - p0], a, b, start=i == 0,
                                                  stop=i == 2)
                            if i == 2 and p1 == n:
                                mm.then_inc(score_full, 1)

            def head(h):
                first = isinstance(h, int) and h == 0
                ta, tb = at_head(h, 12, 7), at_head(h, 2 * T, 4)
                for s in range(steps(h)):
                    x_tiles = X_TILES[s] if first and s < len(X_TILES) else ()
                    projects = lagged(h, s, 0)[0]

                    def part(ks):
                        if s == 0 and not first:
                            pool_project(h - 1, 1, ks)
                        elif projects:
                            project(h, s, ks)
                        elif s > 0:
                            gates(0, *divmod(s - 1, 2), ks=ks)

                    scores_first = projects and s in (1, POOL_STEP + 1)
                    if scores_first:
                        scores(h, s, tb)
                    part(range(3))
                    for t in x_tiles if s else x_tiles[:1]:
                        x_transpose(t)
                    if not scores_first:
                        scores(h, s, tb)
                    there, t, u, _ = lagged(h, s, 3)
                    if there:
                        pe.wait_ge(w_tok_ready, u + 1)
                        wait(pe, tb_free, tb)
                        weights_transpose(t, 0).then_inc(tb_full, 1)
                        tb = tb + 1
                    w_first, w_second = tb, ta
                    part(range(3, 5))
                    if there and t >= 4:
                        wait(pe, ta_free, ta)
                        weights_transpose(t, 1).then_inc(ta_full, 1)
                        ta = ta + 1
                        w_second = ta
                    part(range(5, 8))
                    if first and s == 0:
                        for t in x_tiles[1:]:
                            x_transpose(t)
                        pe.wait_ge(vec_in, 16 * 7)
                        nc.tensor.transpose(bank[:, OUT, 0:N_ROWS], vec_rows[:],
                                            ident[0:N_ROWS, 0:N_ROWS]).then_inc(vec_full, 1)
                    there, t, u, _ = lagged(h, s, 1)
                    if there:
                        pe.wait_ge(qk_normed, u + 1)
                        wait(pe, tb_free, tb)
                        nc.tensor.transpose(bank[:, TB, 0:P], qk_norm[t % 2][:, 0:P], ident[:])
                        nc.tensor.transpose(bank[:, TB, P:2 * P], qk_norm[t % 2][:, P:2 * P],
                                            ident[:]).then_inc(tb_full, 1)
                        tb = tb + 1
                    there, t, u, _ = lagged(h, s, 3)
                    if there:
                        pe.wait_ge(v_ready, u + 1)
                        wait(pe, out_free, u)
                        for k in range(t + 1):
                            if k == 0:
                                pe.wait_ge(tb_free, w_first)
                            if k == 4:
                                pe.wait_ge(ta_free, w_second)
                            hi, lo = (wT[k // 4][i][:, k % 4, :] for i in range(2))
                            wide = (bank[:, OUT, 0:2 * P], hi, v_tok[:, k, :, :].rearrange("p a b -> p (a b)"))
                            narrow = (bank[:, OUT, 0:P], lo, v_tok[:, k, 0, :])
                            for i, m in enumerate((wide, narrow) if k == 0 else (narrow, wide)):
                                mm = nc.tensor.matmul(*m, start=k == 0 and i == 0, stop=k == t and i == 1)
                        mm.then_inc(out_full, 1)
                    there, t, u, _ = lagged(h, s, 4)
                    if there:
                        pe.wait_ge(a_normed, u + 1)
                        wait(pe, ta_free, ta)
                        nc.tensor.transpose(bank[:, TA, 0:P], attn_norm[t % 2][:], ident[:]).then_inc(ta_full, 1)
                        ta = ta + 1
                    if s == POOL_STEP and projects:
                        pool_project(h, 0, range(8))
                    if s == 0 and not first and projects:
                        project(h, 0, range(8))

            pe.wait_ge(ident_ready, 1)
            x_transpose(0)
            head(0)
            with pe.Fori(1, HEADS) as h:
                head(h)

            def up_projection(d, br, i):
                if isinstance(d, int):
                    if br == 0:
                        pe.wait_ge(exp_ready, 2 * T * HEADS)
                        pe.wait_ge(gate_ready, 2)
                        pe.wait_ge(ta_free, 12 * HEADS)
                    else:
                        pe.wait_ge(mix_split, 2 * GROUPS)
                else:
                    pe.wait_ge(gated, 4 * d)
                pe.wait_ge(w_ready, tile_block(d, 2))
                w = wblock(2)
                src = (attnT, mixT)[br]
                passes(bank[:, up_bank(d, 2 * br + i), :], [(cut(w, ALL, 4 * br + k), cut(src, ALL, k, HALVES[i]))
                                                            for k in range(4)]).then_inc(up_full, 1)

            def pool_map(g):
                w = wblock(3)
                n = GROUP_ORDER.index(g)
                if n < 2:
                    pe.wait_ge(w_ready, POOL_W)
                    pe.wait_ge(tb_free, 2 * T * HEADS)
                    pe.wait_ge(ta_free, 12 * HEADS)
                    pe.wait_ge(out_free, T * HEADS)
                    pe.wait_ge(gate_ready, 1)
                pe.wait_ge(pooled_split, n + 1)
                for i in range(2):
                    wait(pe, mix_split, 2 * (n - 2) + i + 1)
                    passes(bank[:, mix_bank(n, i), :], [(cut(w, ALL, g), cut(mixT, ALL, g, HALVES[i]))]).then_inc(mix_full, 1)

            head(HEADS)
            gates(0, 1, 1)
            pool_map(0)
            pool_map(1)
            up_projection(0, 0, 0)
            pool_map(3)
            up_projection(0, 0, 1)
            pool_map(2)
            up_projection(0, 1, 0)
            up_projection(0, 1, 1)
            with pe.Fori(1, KD) as d:
                for g in range(2):
                    gates(d, g, 0)
                    gates(d, g, 1)
                for i in range(2):
                    up_projection(d, 0, i)
                    up_projection(d, 1, i)

            def out_projection(t):
                wait(pe, m_split, t)
                for i in range(2):
                    n = 2 * t + i
                    if t == 0:
                        pe.wait_ge(gate_ready, 4 * KD)
                    wait(pe, res_ready, n - 3)
                    for k in range(KD):
                        if t == 0:
                            if k % 2 == 0:
                                pe.wait_ge(w_ready, WO + 4 * i + k // 2)
                            pe.wait_ge(m_first, 1 + (k == KD - 1))
                        w = (k4(slots[4 * i + k // 2][0], 2), k4(slots[4 * i + k // 2][1], 2))
                        mm = passes(bank[:, n % 4, :], [(cut(featT, ALL, k, slice(t * P, (t + 1) * P)), cut(w, ALL, k % 2))],
                                    start=k == 0, stop=k == KD - 1)
                    mm.then_inc(wo_full, 1)

            def h2_transpose(t):
                pe.wait_ge(h2_ready, t + 1)
                if t < 2:
                    pe.wait_ge(gated, 4 * KD)
                for b in range(2):
                    wait(pe, h2T_split, 2 * (t - 2) + b + 1)
                    for k in range(4):
                        kk = 4 * b + k
                        mm = nc.tensor.transpose(bank[:, 4 + 2 * (t % 2) + b, k * P:(k + 1) * P],
                                                 h2_row[t % 2][:, kk * P:(kk + 1) * P], ident[:])
                    mm.then_inc(h2T_full, 1)

            for t in range(T):
                out_projection(t)
                if t > 1:
                    h2_transpose(t - 2)

            def mlp_up(c):
                first = isinstance(c, int)
                for q, (j, i) in enumerate(up_order(c)):
                    pe.wait_ge(w_ready, MLP0 + 8 * c + mlp_pos["in", j])
                    w = tuple(k4(part, 8) for part in mlp_slot("in", j))
                    if first and q == 0:
                        pe.wait_ge(res_ready, 2 * T)
                        h2_transpose(T - 2)
                        pe.wait_ge(h2T_split, T)
                    if first and q == 1:
                        h2_transpose(T - 1)
                    if first and q == 2:
                        pe.wait_ge(h2T_split, 2 * T)
                    wait(pe, relu_ready, 8 * c + q - 3)
                    passes(bank[:, q % 4, :], [(cut(w, ALL, k), cut(featT, ALL, k, HALVES[i]))
                                               for k in range(KD)]).then_inc(u_done, 1)

            def mlp_down(c):
                pe.wait_ge(w_ready, MLP0 + 8 * c + 7)
                for t in range(T):
                    for i, half in enumerate(HALVES):
                        n = 2 * t + i
                        if n == 0:
                            pe.wait_ge(u_split, 8 * c + 4)
                        elif n > 3:
                            pe.wait_ge(y_added, 2 * T * c + n - 3)
                        pairs = [(cut(uT, ALL, j, slice(t * P, (t + 1) * P)),
                                  (slots[j][0][:, half], slots[j][1][:, half])) for j in range(CH)]
                        if t in (0, T // 2) and i == 0:
                            passes(bank[:, 4 + n % 4, :], pairs[:-1], stop=False)
                            pe.wait_ge(u_split, 8 * c + (7 if t == 0 else 8))
                            mm = passes(bank[:, 4 + n % 4, :], pairs[-1:], start=False)
                        else:
                            mm = passes(bank[:, 4 + n % 4, :], pairs)
                        mm.then_inc(down_full, 1)

            mlp_up(0)
            with pe.Fori(1, CHUNKS) as c:
                mlp_down(c - 1)
                mlp_up(c)
            mlp_down(CHUNKS - 1)


_INS = ["x", "norm1_g", "w_in", "b_gate", "q_norm_g", "k_norm_g", "lam_params", "subln_g", "pool_w", "pool_scale",
        "w_up_attn", "w_up_pool", "w_o", "norm2_g", "w_mlp_in", "w_mlp_out"]


def kernel(**inputs):
    import numpy as np
    import concourse.bacc as bacc
    from concourse.bass_utils import run_bass_kernel_spmd

    nc = bacc.Bacc("TRN2", target_bir_lowering=False, num_devices=1, dynamic_dma_scratch_size=1024)
    arrays, args = {}, []
    for name in _INS:
        a = np.ascontiguousarray(inputs[name])
        arrays[f"in_{name}"] = a
        args.append(nc.dram_tensor(f"in_{name}", a.shape, mybir.dt.from_np(a.dtype), kind="ExternalInput").ap())
    args.append(nc.dram_tensor("out_y", inputs["x"].shape, F32, kind="ExternalOutput").ap())
    trunk_layer(nc, *args)
    r = run_bass_kernel_spmd(nc, [arrays], core_ids=[0])
    return r.results[0]["out_y"]
```
